# Optimizing a Trainium2 kernel written in Bass

```python
import jax, jax.numpy as jnp
from jax import lax
import numpy as np

D_MODEL = 1024
BATCH = 1
SEQ = 2048
DEPTH = 1
DEC_BATCH = 1
DEC_SEQ = 32
PAST_LEN = 256

CHUNK = 64
D_CONV = D_MODEL // 2
D_LRU = D_MODEL - D_CONV
N_LRU_HEADS = 8
LRU_HEAD_DIM = D_LRU // N_LRU_HEADS
CONV_A_WIDTH = 3
CONV_B_WIDTH = 4
LRU_C = 8.0
N_GROUPS = 4
EXPERTS_PER_GROUP = 4
N_EXPERTS = N_GROUPS * EXPERTS_PER_GROUP
TOP_K_INNER = 2
D_EXPERT = D_MODEL // 4
D_IN_PROJ = 3 * D_CONV + 2 * D_LRU
ALPHA = (2.0 * DEPTH) ** 0.25
BETA = (8.0 * DEPTH) ** -0.25
LN_EPS = 1e-5

kernel_name = "hybrid_conv_rglru_hiermoe_stream_step"

def layer_norm(x, g, b):
    xf = x.astype(jnp.float32)
    mu = jnp.mean(xf, axis=-1, keepdims=True)
    var = jnp.mean(jnp.square(xf - mu), axis=-1, keepdims=True)
    return ((xf - mu) * lax.rsqrt(var + LN_EPS) * g.astype(jnp.float32)
            + b.astype(jnp.float32)).astype(x.dtype)

def causal_depthwise_conv(u, prev, w):
    width = w.shape[0]
    T = u.shape[1]
    up = jnp.concatenate([prev.astype(u.dtype), u], axis=1)
    y = up[:, 0:T] * w[0]
    for k in range(1, width):
        y = y + up[:, k:k + T] * w[k]
    return y, up[:, up.shape[1] - (width - 1):]

def rg_lru(xc, h_prev, wa, ba, wx, bx, lam):
    bsz, T, _ = xc.shape
    xh = xc.reshape(bsz, T, N_LRU_HEADS, LRU_HEAD_DIM)
    r = jax.nn.sigmoid(jnp.einsum('bthi,hij->bthj', xh, wa).reshape(bsz, T, D_LRU) + ba)
    i = jax.nn.sigmoid(jnp.einsum('bthi,hij->bthj', xh, wx).reshape(bsz, T, D_LRU) + bx)
    log_a = -LRU_C * r.astype(jnp.float32) * jax.nn.softplus(-lam.astype(jnp.float32))
    a = jnp.exp(log_a)
    b = jnp.sqrt(-jnp.expm1(2.0 * log_a)) * (i * xc).astype(jnp.float32)
    b = b.at[:, 0].add(a[:, 0] * h_prev.astype(jnp.float32))

    def combine(left, right):
        a1, b1 = left
        a2, b2 = right
        return a1 * a2, a2 * b1 + b2

    _, h = lax.associative_scan(combine, (a, b), axis=1)
    return h.astype(xc.dtype), h[:, -1].astype(h_prev.dtype)

def hybrid_mixer(x, conv_a_prev, conv_b_prev, h_prev, w_in, conv_a_w, conv_b_w,
                 conv_b_bias, lru_wa, lru_ba, lru_wx, lru_bx, lru_lambda, w_out):
    proj = x @ w_in
    gate_b, gate_c, val_a, val_b, gate_lru = jnp.split(
        proj, [D_CONV, 2 * D_CONV, 3 * D_CONV, 3 * D_CONV + D_LRU], axis=-1)
    u = gate_c * val_a
    uc, new_conv_a = causal_depthwise_conv(u, conv_a_prev, conv_a_w)
    y_a = gate_b * uc
    xc, new_conv_b = causal_depthwise_conv(val_b, conv_b_prev, conv_b_w)
    xc = xc + conv_b_bias
    h, new_h = rg_lru(xc, h_prev, lru_wa, lru_ba, lru_wx, lru_bx, lru_lambda)
    y_b = h * jax.nn.gelu(gate_lru)
    out = jnp.concatenate([y_a, y_b], axis=-1) @ w_out
    return out, new_conv_a.astype(conv_a_prev.dtype), new_conv_b.astype(conv_b_prev.dtype), new_h

def hier_moe(x, w_router_group, w_router_expert, moe_w1, moe_w3, moe_w2):
    shp = x.shape
    xt = x.reshape(-1, D_MODEL)
    p_grp = jax.nn.softmax((xt @ w_router_group).astype(jnp.float32), axis=-1)
    g_idx = jnp.argmax(p_grp, axis=-1)
    g_gate = jnp.take_along_axis(p_grp, g_idx[:, None], axis=-1)
    e_logits = (xt @ w_router_expert).astype(jnp.float32).reshape(-1, N_GROUPS, EXPERTS_PER_GROUP)
    e_logits = jnp.take_along_axis(e_logits, g_idx[:, None, None], axis=1)[:, 0]
    top_v, top_i = lax.top_k(e_logits, TOP_K_INNER)
    top_w = jax.nn.softmax(top_v, axis=-1) * g_gate
    expert_id = g_idx[:, None] * EXPERTS_PER_GROUP + top_i
    gates = jnp.sum(jax.nn.one_hot(expert_id, N_EXPERTS, dtype=jnp.float32)
                    * top_w[..., None], axis=1)
    h = jax.nn.silu(jnp.einsum('nd,edf->nef', xt, moe_w1)) * jnp.einsum('nd,edf->nef', xt, moe_w3)
    h = h * gates.astype(h.dtype)[..., None]
    y = jnp.einsum('nef,efd->nd', h, moe_w2)
    return y.reshape(shp)

def trunk_layer(x, conv_a_prev, conv_b_prev, h_prev, ln1_g, ln1_b, w_in, conv_a_w,
                conv_b_w, conv_b_bias, lru_wa, lru_ba, lru_wx, lru_bx, lru_lambda, w_out,
                ln2_g, ln2_b, w_router_group, w_router_expert, moe_w1, moe_w3, moe_w2):
    m, nca, ncb, nh = hybrid_mixer(x, conv_a_prev, conv_b_prev, h_prev, w_in, conv_a_w,
                                   conv_b_w, conv_b_bias, lru_wa, lru_ba, lru_wx, lru_bx,
                                   lru_lambda, w_out)
    x = layer_norm(ALPHA * x + m, ln1_g, ln1_b)
    x = layer_norm(ALPHA * x + hier_moe(x, w_router_group, w_router_expert, moe_w1, moe_w3, moe_w2),
                   ln2_g, ln2_b)
    return x, nca, ncb, nh

def setup_inputs(seed: int = 0) -> dict:
    key = jax.random.key(seed)
    ks = jax.random.split(key, 24)
    f32 = jnp.float32
    nrm = lambda k, shp, s: jax.random.normal(k, shp, f32) * s
    L = DEPTH
    u = jax.random.uniform(ks[13], (L, D_LRU), f32, 0.9, 0.999)
    a_base = u ** (1.0 / LRU_C)
    return {
        "x_prompt": nrm(ks[0], (BATCH, SEQ, D_MODEL), 1.0),
        "x_sample": nrm(ks[1], (DEC_BATCH, DEC_SEQ, D_MODEL), 1.0),
        "state_conv_a": nrm(ks[2], (L, DEC_BATCH, CONV_A_WIDTH - 1, D_CONV), 1.0),
        "state_conv_b": nrm(ks[3], (L, DEC_BATCH, CONV_B_WIDTH - 1, D_LRU), 1.0),
        "state_lru_h": nrm(ks[4], (L, DEC_BATCH, D_LRU), 0.5),
        "ln1_g": 1.0 + nrm(ks[5], (L, D_MODEL), 0.02),
        "ln1_b": nrm(ks[6], (L, D_MODEL), 0.02),
        "w_in": nrm(ks[7], (L, D_MODEL, D_IN_PROJ), D_MODEL ** -0.5),
        "conv_a_w": nrm(ks[8], (L, CONV_A_WIDTH, D_CONV), CONV_A_WIDTH ** -0.5),
        "conv_b_w": nrm(ks[9], (L, CONV_B_WIDTH, D_LRU), CONV_B_WIDTH ** -0.5),
        "conv_b_bias": nrm(ks[10], (L, D_LRU), 0.02),
        "lru_wa": nrm(ks[11], (L, N_LRU_HEADS, LRU_HEAD_DIM, LRU_HEAD_DIM), LRU_HEAD_DIM ** -0.5),
        "lru_ba": nrm(ks[12], (L, D_LRU), 0.1),
        "lru_wx": nrm(ks[14], (L, N_LRU_HEADS, LRU_HEAD_DIM, LRU_HEAD_DIM), LRU_HEAD_DIM ** -0.5),
        "lru_bx": nrm(ks[15], (L, D_LRU), 0.1),
        "lru_lambda": jnp.log(a_base) - jnp.log1p(-a_base),
        "w_out": nrm(ks[16], (L, D_MODEL, D_MODEL), BETA * D_MODEL ** -0.5),
        "ln2_g": 1.0 + nrm(ks[17], (L, D_MODEL), 0.02),
        "ln2_b": nrm(ks[18], (L, D_MODEL), 0.02),
        "w_router_group": nrm(ks[19], (L, D_MODEL, N_GROUPS), D_MODEL ** -0.5),
        "w_router_expert": nrm(ks[20], (L, D_MODEL, N_EXPERTS), D_MODEL ** -0.5),
        "moe_w1": nrm(ks[21], (L, N_EXPERTS, D_MODEL, D_EXPERT), D_MODEL ** -0.5),
        "moe_w3": nrm(ks[22], (L, N_EXPERTS, D_MODEL, D_EXPERT), D_MODEL ** -0.5),
        "moe_w2": nrm(ks[23], (L, N_EXPERTS, D_EXPERT, D_MODEL), BETA * D_EXPERT ** -0.5),
    }

def reference(x_prompt, x_sample, state_conv_a, state_conv_b, state_lru_h, ln1_g, ln1_b,
              w_in, conv_a_w, conv_b_w, conv_b_bias, lru_wa, lru_ba, lru_wx, lru_bx,
              lru_lambda, w_out, ln2_g, ln2_b, w_router_group, w_router_expert,
              moe_w1, moe_w3, moe_w2):
    bp = x_prompt.shape[0]
    yp, ys = x_prompt, x_sample
    ca_p, cb_p, h_p, ca_s, cb_s, h_s = [], [], [], [], [], []
    for l in range(DEPTH):
        w = (ln1_g[l], ln1_b[l], w_in[l], conv_a_w[l], conv_b_w[l], conv_b_bias[l],
             lru_wa[l], lru_ba[l], lru_wx[l], lru_bx[l], lru_lambda[l], w_out[l],
             ln2_g[l], ln2_b[l], w_router_group[l], w_router_expert[l],
             moe_w1[l], moe_w3[l], moe_w2[l])
        yp, a1, b1, h1 = trunk_layer(
            yp,
            jnp.zeros((bp, CONV_A_WIDTH - 1, D_CONV), state_conv_a.dtype),
            jnp.zeros((bp, CONV_B_WIDTH - 1, D_LRU), state_conv_b.dtype),
            jnp.zeros((bp, D_LRU), state_lru_h.dtype), *w)
        ys, a2, b2, h2 = trunk_layer(ys, state_conv_a[l], state_conv_b[l], state_lru_h[l], *w)
        ca_p.append(a1); cb_p.append(b1); h_p.append(h1)
        ca_s.append(a2); cb_s.append(b2); h_s.append(h2)
    return (yp, ys, jnp.stack(ca_p), jnp.stack(cb_p), jnp.stack(h_p),
            jnp.stack(ca_s), jnp.stack(cb_s), jnp.stack(h_s))


_drawn_inputs = setup_inputs


def setup_inputs(seed=0):
    import zlib

    import numpy as np

    out = dict(_drawn_inputs(seed))
    spreads = {}
    factors = {}
    for name, (base, spread) in spreads.items():
        noise = np.random.default_rng([zlib.crc32(name.encode()), seed]).standard_normal(out[name].shape)
        drawn = base * np.exp(spread * noise) if base else spread * noise
        out[name] = __import__('jax').numpy.asarray(drawn.astype(out[name].dtype))
    for name, factor in factors.items():
        out[name] = (out[name] * factor).astype(out[name].dtype)
    return out
```

```python
from contextlib import ExitStack

import concourse.bass as bass
from concourse import mybir

F32 = mybir.dt.float32
F32R = mybir.dt.float32r
I32 = mybir.dt.int32
ALU = mybir.AluOpType
ACT = mybir.ActivationFunctionType
AX = mybir.AxisListType

P = 128
D = 1024
KT = D // P
SEQ, DEC = 2048, 32
TOK = SEQ + DEC
CHUNK = 416
NCH = TOK // CHUNK
HEAD = SEQ - (NCH - 1) * CHUNK
GAP = 3
EXT = HEAD + GAP + DEC
LRU_N = EXT + 1
GROUPS = 4
MT = 5
WP = MT + 1
XP = KT // 2
NT = -(-TOK // P)
TAIL = TOK - (NT - 1) * P
ROWS = NT * P
NG, NE_G, NE = 4, 4, 16
FE = 256
FT = FE // P
TOPK = 2
STEPS = (TOPK * TOK + NE * P) // P
NR = NG + NE
ALPHA = 2.0 ** 0.25
LN_EPS = 1e-5
GELU_A, GELU_B = 0.7978845608028654, 0.7978845608028654 * 0.044715
(CA0, CA1, CA2, CB0, CB1, CB2, CB3, CBIAS, RBIAS, IBIAS, LAM, HA0, HA1, HB0, HB1, HB2, HPREV, NCOL) = range(18)
SA_P, SB_P, SA_S, SB_S, SH_P, SH_S, NST = 0, 2, 5, 7, 10, 11, 12
C_ID, C_TRI, C_ONE, C_IO = 0, P, 2 * P, 3 * P
C_DEC = 4 * P
C_THR, C_TOK, C_VAL, C_INV = (C_DEC + NG + NT * i for i in range(4))
C_SEG = C_INV + NT
C_PAD = C_SEG + NT * NE
NCONST = C_PAD + 1


def mixer_phase(nc, x_t, w_in, w_lru, chan, y_scr, states):
    with ExitStack() as ctx:
        def sb(name, shape, dt=F32):
            return ctx.enter_context(nc.sbuf_tensor(name, shape, dt))

        def sem(name):
            return ctx.enter_context(nc.semaphore(name))

        x_hi = sb("x_hi", [P, KT, TOK], F32R)
        x_lo = sb("x_lo", [P, KT, TOK], F32R)
        w_hi = sb("w_hi", [P, MT, KT, P], F32R)
        w_lo = sb("w_lo", [P, MT, KT, P], F32R)
        l_hi = sb("l_hi", [P, 2, P], F32R)
        l_lo = sb("l_lo", [P, 2, P], F32R)
        w_raw = sb("w_raw", [P, 2, KT, P])
        x_raw = sb("x_raw", [P, 2, 2, CHUNK])
        par = sb("par", [P, GROUPS, NCOL])
        vb = sb("vb", [P, 3 + EXT + 2])
        u = sb("u", [P, 2 + EXT + 1])
        xc = sb("xc", [P, LRU_N])
        xc_hi = sb("xc_hi", [P, LRU_N], F32R)
        xc_lo = sb("xc_lo", [P, LRU_N], F32R)
        gate_c = sb("gate_c", [P, CHUNK])
        ya = sb("ya", [P, EXT + 1])
        gel = sb("gel", [P, CHUNK])
        yb = sb("yb", [P, LRU_N])
        a_t = sb("a_t", [P, LRU_N])
        b_t = sb("b_t", [P, LRU_N])
        i_t = sb("i_t", [P, LRU_N])
        h_carry = sb("h_carry", [P, 1])
        stash = sb("stash", [P, GROUPS, NST])
        sp4 = sb("sp4", [P, GROUPS])
        nsp4 = sb("nsp4", [P, GROUPS])
        hrb = sb("hrb", [P, GROUPS])
        hib = sb("hib", [P, GROUPS])
        sp_t = sb("sp_t", [P, 8, GROUPS])

        ps = [ctx.enter_context(nc.psum_tensor(f"ps_{n}", [P, 512], F32))
              for n in ("vb", "c", "va", "b", "g", "r", "i")]
        ps_vb, ps_c, ps_va, ps_b, ps_g, ps_r, ps_i = ps

        s_par = sem("s_par")
        s_wraw = [sem(f"s_wraw{i}") for i in range(2)]
        s_xraw = [sem(f"s_xraw{i}") for i in range(2)]
        s_whi, s_wlo = sem("s_whi"), sem("s_wlo")
        s_xhi, s_xlo = sem("s_xhi"), sem("s_xlo")
        s_mm = [sem(f"s_mm{i}") for i in range(MT)]
        s_ri = sem("s_ri")
        s_vb = sem("s_vb")
        s_hist = sem("s_hist")
        s_tapb = sem("s_tapb")
        s_convb = sem("s_convb")
        s_xch, s_xcl = sem("s_xch"), sem("s_xcl")
        s_c = sem("s_c")
        s_u = sem("s_u")
        s_tapa = sem("s_tapa")
        s_conva = sem("s_conva")
        s_ya = sem("s_ya")
        s_ya_out, s_yb_out = sem("s_ya_out"), sem("s_yb_out")
        s_gsq, s_gp, s_gt, s_gel = sem("s_gsq"), sem("s_gp"), sem("s_gt"), sem("s_gel")
        s_thr, s_thi = sem("s_thr"), sem("s_thi")
        s_a, s_t = sem("s_a"), sem("s_t")
        s_z, s_sq = sem("s_z"), sem("s_sq")
        s_m = sem("s_m")
        s_b = sem("s_b")
        s_fix = sem("s_fix")
        s_h = sem("s_h")
        s_yb = sem("s_yb")
        s_sp = sem("s_sp")
        s_spe = sem("s_spe")
        s_tail = sem("s_tail")
        s_carry = sem("s_carry")
        s_st = sem("s_st")
        s_st_out = sem("s_st_out")

        def segs(last):
            return [(0, 0, HEAD), (HEAD, HEAD + GAP, DEC)] if last else [(0, 0, CHUNK)]

        block = ctx.enter_context(nc.Block())

        @block.gpsimd
        def _(pool):
            pool.dma_start(par[:], chan).then_inc(s_par, 16)
            for i in range(WP):
                if i >= 2:
                    pool.wait_ge(s_wlo, i - 1)
                dst = w_raw[:, i % 2] if i < MT else w_raw[:, i % 2, 0:2]
                src = w_in[i] if i < MT else w_lru[0]
                pool.dma_start(dst, src).then_inc(s_wraw[i % 2], 16)
            with pool.Fori(1, GROUPS) as j:
                for i in range(WP):
                    pool.wait_ge(s_wlo, j * WP + (i - 1))
                    if i < MT:
                        pool.dma_start(w_raw[:, i % 2],
                                       w_in[bass.ds(j * MT + i, 1)].rearrange("o p k n -> p (o k) n")).then_inc(s_wraw[i % 2], 16)
                    else:
                        pool.dma_start(w_raw[:, i % 2, 0:2],
                                       w_lru[bass.ds(j, 1)].rearrange("o p k n -> p (o k) n")).then_inc(s_wraw[i % 2], 16)

        @block.sync
        def _(sp):
            def load_x(c, first):
                for n in range(XP):
                    if not (first and n < 2):
                        sp.wait_ge(s_xlo, c * XP + (n - 1))
                    sp.dma_start(x_raw[:, n % 2], x_t[:, 2 * n:2 * n + 2, bass.ds(c * CHUNK, CHUNK)]).then_inc(s_xraw[n % 2], 16)

            def store_y(j, c, last):
                q = j * NCH + c
                for src, s_ready, s_out, half in ((ya, s_ya, s_ya_out, 0), (yb, s_yb, s_yb_out, GROUPS)):
                    sp.wait_ge(s_ready, q + 1)
                    row = y_scr[bass.ds(j + half, 1)].rearrange("o p t -> p (o t)")
                    if last:
                        sp.dma_start(row[:, SEQ - HEAD:SEQ], src[:, 0:HEAD]).then_inc(s_out, 16)
                        sp.dma_start(row[:, SEQ:TOK], src[:, HEAD + GAP:EXT]).then_inc(s_out, 16)
                    else:
                        sp.dma_start(row[:, bass.ds(c * CHUNK, CHUNK)], src[:, 0:CHUNK]).then_inc(s_out, 16)

            load_x(0, True)
            with sp.Fori(0, NCH - 1) as c:
                load_x(c + 1, False)
                store_y(0, c, False)
            store_y(0, NCH - 1, True)
            with sp.Fori(1, GROUPS) as j:
                with sp.Fori(0, NCH - 1) as c:
                    store_y(j, c, False)
                store_y(j, NCH - 1, True)
            sp.wait_ge(s_st, GROUPS)
            sp.dma_start(states, stash[:]).then_inc(s_st_out, 16)
            sp.wait_ge(s_st_out, 16)
            sp.wait_ge(s_ya_out, 16 * GROUPS * (NCH + 1))
            sp.wait_ge(s_yb_out, 16 * GROUPS * (NCH + 1))

        @block.tensor
        def _(pe):
            def step(j, c):
                q = j * NCH + c
                pe.wait_ge(s_xlo, (c + 1) * XP)
                free = (s_vb, s_c, s_u, s_ya, s_gel)
                for i in range(MT):
                    pe.wait_ge(s_wlo, j * WP + (i + 1))
                    pe.wait_ge(free[i], q)
                    for k in range(KT):
                        for n, (w, x) in enumerate(((w_hi, x_hi), (w_hi, x_lo), (w_lo, x_hi))):
                            mm = pe.matmul(ps[i][:, 0:CHUNK], w[:, i, k], x[:, k, bass.ds(c * CHUNK, CHUNK)],
                                           start=(k == 0 and n == 0), stop=(k == KT - 1 and n == 2))
                    mm.then_inc(s_mm[i], 1)
                pe.wait_ge(s_wlo, j * WP + WP)
                pe.wait_ge(s_xcl, q + 1)
                pe.wait_ge(s_thi, q)
                for g, bank in enumerate((ps_r, ps_i)):
                    for n, (w, x) in enumerate(((l_hi, xc_hi), (l_hi, xc_lo), (l_lo, xc_hi))):
                        mm = pe.matmul(bank[:, 0:LRU_N], w[:, g], x[:], start=(n == 0), stop=(n == 2))
                mm.then_inc(s_ri, 1)

            step(0, 0)
            with pe.Fori(1, NCH) as c:
                step(0, c)
            with pe.Fori(1, GROUPS) as j:
                with pe.Fori(0, NCH) as c:
                    step(j, c)

        def raw_piece(i):
            return (w_raw[:, i % 2], w_hi[:, i], w_lo[:, i]) if i < MT else (w_raw[:, i % 2, 0:2], l_hi[:], l_lo[:])

        @block.scalar
        def _(act):
            def split_w(j, i):
                raw, hi, _ = raw_piece(i)
                act.wait_ge(s_wraw[i % 2], 16 * (j * (WP // 2) + (i // 2 + 1)))
                act.wait_ge(s_mm[i] if i < MT else s_ri, j * NCH)
                act.activation(hi, raw, ACT.Copy).then_inc(s_whi, 1)

            def split_x(c, n):
                act.wait_ge(s_xraw[n % 2], 16 * (c * (XP // 2) + (n // 2 + 1)))
                act.activation(x_hi[:, 2 * n:2 * n + 2, bass.ds(c * CHUNK, CHUNK)], x_raw[:, n % 2], ACT.Copy).then_inc(s_xhi, 1)

            def step(j, c, last, split):
                q = j * NCH + c
                col = lambda n: par[:, bass.ds(j, 1), n]
                act.wait_ge(s_mm[0], q + 1)
                act.wait_ge(s_hist, q + 1)
                for k, (s, d, n) in enumerate(segs(last)):
                    ins = act.activation(vb[:, 3 + d:3 + d + n], ps_vb[:, s:s + n], ACT.Copy)
                ins.then_inc(s_vb, 1)
                if split is not None:
                    split(0)
                n = EXT if last else CHUNK
                act.wait_ge(s_vb, q + 1)
                act.wait_ge(s_m, q)
                act.activation(xc[:, 0:n], vb[:, 0:n], ACT.Identity, scale=col(CB0), bias=col(CBIAS)).then_inc(s_tapb, 1)
                act.wait_ge(s_mm[1], q + 1)
                act.wait_ge(s_u, q)
                act.activation(gate_c[:], ps_c[:, 0:CHUNK], ACT.Copy).then_inc(s_c, 1)
                if split is not None:
                    split(1)
                act.wait_ge(s_convb, 3 * q + 3)
                act.wait_ge(s_ri, q)
                act.activation(xc_hi[:], xc[:], ACT.Copy).then_inc(s_xch, 1)
                act.wait_ge(s_u, q + 1)
                act.wait_ge(s_ya_out, 16 * (q + j))
                act.activation(ya[:, 0:n], u[:, 0:n], ACT.Copy, scale=col(CA0)).then_inc(s_tapa, 1)
                if split is not None:
                    split(2)
                    split(3)
                act.wait_ge(s_mm[4], q + 1)
                act.wait_ge(s_yb, q)
                act.activation(gel[:], ps_g[:, 0:CHUNK], ACT.Square).then_inc(s_gsq, 1)
                act.wait_ge(s_gp, 2 * q + 2)
                act.activation(gel[:], gel[:], ACT.Tanh).then_inc(s_gt, 1)
                if split is not None:
                    split(4)
                act.wait_ge(s_ri, q + 1)
                act.wait_ge(s_yb_out, 16 * (q + j))
                act.activation(yb[:], ps_r[:, 0:LRU_N], ACT.Tanh, scale=0.5, bias=hrb[:, bass.ds(j, 1)]).then_inc(s_thr, 1)
                act.wait_ge(s_b, q)
                act.activation(i_t[:], ps_i[:, 0:LRU_N], ACT.Tanh, scale=0.5, bias=hib[:, bass.ds(j, 1)]).then_inc(s_thi, 1)
                act.wait_ge(s_thr, q + 1)
                act.wait_ge(s_h, q)
                act.activation(a_t[:], yb[:], ACT.Exp, scale=nsp4[:, bass.ds(j, 1)], bias=nsp4[:, bass.ds(j, 1)]).then_inc(s_a, 1)
                act.wait_ge(s_a, q + 1)
                act.activation(yb[:], yb[:], ACT.Tanh, scale=sp4[:, bass.ds(j, 1)], bias=sp4[:, bass.ds(j, 1)]).then_inc(s_t, 1)
                if split is not None:
                    split(5)
                act.wait_ge(s_z, 2 * q + 2)
                act.activation(yb[:], yb[:], ACT.Sqrt).then_inc(s_sq, 1)

            act.wait_ge(s_sp, 1)
            act.activation(sp_t[:, 1], sp_t[:, 0], ACT.Exp, scale=-1.0).then_inc(s_spe, 1)
            split_w(0, 0)
            for n in range(XP):
                split_x(0, n)
            for i in range(1, WP):
                split_w(0, i)
            act.wait_ge(s_sp, 15)
            for n in range(XP):
                split_x(1, n)
            step(0, 0, False, None)
            with act.Fori(1, NCH - 1) as c:
                for n in range(XP):
                    split_x(c + 1, n)
                step(0, c, False, None)
            step(0, NCH - 1, True, lambda i: split_w(1, i))
            with act.Fori(1, GROUPS - 1) as j:
                with act.Fori(0, NCH - 1) as c:
                    step(j, c, False, None)
                step(j, NCH - 1, True, lambda i: split_w(j + 1, i))
            with act.Fori(0, NCH - 1) as c:
                step(GROUPS - 1, c, False, None)
            step(GROUPS - 1, NCH - 1, True, None)

        @block.vector
        def _(dve):
            def split_w(j, i):
                raw, hi, lo = raw_piece(i)
                dve.wait_ge(s_whi, j * WP + (i + 1))
                dve.tensor_tensor(lo, raw, hi.bitcast(F32), ALU.subtract).then_inc(s_wlo, 1)

            def split_x(c, n):
                dve.wait_ge(s_xhi, c * XP + (n + 1))
                at = bass.ds(c * CHUNK, CHUNK)
                dve.tensor_tensor(x_lo[:, 2 * n:2 * n + 2, at], x_raw[:, n % 2],
                                  x_hi[:, 2 * n:2 * n + 2, at].bitcast(F32), ALU.subtract).then_inc(s_xlo, 1)

            def step(j, c, last, split):
                q = j * NCH + c
                n = EXT if last else CHUNK
                col = lambda m: par[:, bass.ds(j, 1), m]
                if split is not None:
                    split(0)
                for k in range(1, 4):
                    if k == 1:
                        dve.wait_ge(s_tapb, q + 1)
                    else:
                        dve.wait_ge(s_convb, 3 * q + (k - 1))
                    dve.scalar_tensor_tensor(out=xc[:, 0:n], in0=vb[:, k:k + n], scalar=col(CB0 + k), in1=xc[:, 0:n],
                                             op0=ALU.mult, op1=ALU.add).then_inc(s_convb, 1)
                if split is not None:
                    split(1)
                dve.wait_ge(s_xch, q + 1)
                dve.tensor_tensor(xc_lo[:], xc[:], xc_hi[:].bitcast(F32), ALU.subtract).then_inc(s_xcl, 1)
                dve.wait_ge(s_c, q + 1)
                dve.wait_ge(s_mm[2], q + 1)
                dve.wait_ge(s_hist, q + 1)
                for s, d, m in segs(last):
                    ins = dve.tensor_tensor(u[:, 2 + d:2 + d + m], ps_va[:, s:s + m], gate_c[:, s:s + m], ALU.mult)
                ins.then_inc(s_u, 1)
                for k in range(1, 3):
                    if k == 1:
                        dve.wait_ge(s_tapa, q + 1)
                    else:
                        dve.wait_ge(s_conva, 2 * q + 1)
                    dve.scalar_tensor_tensor(out=ya[:, 0:n], in0=u[:, k:k + n], scalar=col(CA0 + k), in1=ya[:, 0:n],
                                             op0=ALU.mult, op1=ALU.add).then_inc(s_conva, 1)
                if split is not None:
                    split(2)
                    split(3)
                dve.wait_ge(s_mm[3], q + 1)
                dve.wait_ge(s_conva, 2 * q + 2)
                for s, d, m in segs(last):
                    ins = dve.tensor_tensor(ya[:, d:d + m], ya[:, d:d + m], ps_b[:, s:s + m], ALU.mult)
                ins.then_inc(s_ya, 1)
                if last:
                    st = lambda a, m: stash[:, bass.ds(j, 1), a:a + m].rearrange("p o m -> p (o m)")
                    dve.tensor_copy(st(SA_P, 2), u[:, HEAD:HEAD + 2])
                    dve.tensor_copy(st(SA_S, 2), u[:, EXT:EXT + 2])
                    dve.tensor_copy(st(SB_P, 3), vb[:, HEAD:HEAD + 3])
                    dve.tensor_copy(st(SB_S, 3), vb[:, EXT:EXT + 3]).then_inc(s_tail, 1)
                    dve.wait_ge(s_tail, q + 1)
                    dve.memset(u[:, 0:2], 0.0)
                    dve.memset(vb[:, 0:3], 0.0).then_inc(s_hist, 1)
                else:
                    dve.tensor_copy(u[:, 0:2], u[:, CHUNK:CHUNK + 2])
                    dve.tensor_copy(vb[:, 0:3], vb[:, CHUNK:CHUNK + 3]).then_inc(s_tail, 1)
                    dve.wait_ge(s_tail, q + 1)
                    grp = lambda a, m: par[:, bass.ds(j, 1), a:a + m].rearrange("p o m -> p (o m)")
                    dve.tensor_copy(u[:, HEAD + 2:HEAD + 3], grp(HA0, 1))
                    dve.tensor_copy(u[:, HEAD + 3:HEAD + 5], grp(HA0, 2))
                    dve.tensor_copy(vb[:, HEAD + 3:HEAD + 6], grp(HB0, 3)).then_inc(s_hist, 1)
                dve.wait_ge(s_gsq, q + 1)
                dve.tensor_scalar(gel[:], gel[:], GELU_B, GELU_A, ALU.mult, ALU.add).then_inc(s_gp, 1)
                dve.wait_ge(s_gp, 2 * q + 1)
                dve.tensor_tensor(gel[:], gel[:], ps_g[:, 0:CHUNK], ALU.mult).then_inc(s_gp, 1)
                if split is not None:
                    split(4)
                dve.wait_ge(s_gt, q + 1)
                dve.scalar_tensor_tensor(out=gel[:], in0=gel[:], scalar=1.0, in1=ps_g[:, 0:CHUNK],
                                         op0=ALU.add, op1=ALU.mult).then_inc(s_gel, 1)
                dve.wait_ge(s_a, q + 1)
                dve.tensor_tensor(b_t[:], a_t[:], a_t[:], ALU.mult).then_inc(s_z, 1)
                dve.wait_ge(s_z, 2 * q + 1)
                dve.wait_ge(s_t, q + 1)
                dve.scalar_tensor_tensor(out=yb[:], in0=b_t[:], scalar=1.0, in1=yb[:],
                                         op0=ALU.add, op1=ALU.mult).then_inc(s_z, 1)
                dve.wait_ge(s_thi, q + 1)
                dve.scalar_tensor_tensor(out=i_t[:], in0=i_t[:], scalar=1.0, in1=xc[:],
                                         op0=ALU.add, op1=ALU.mult).then_inc(s_m, 1)
                if split is not None:
                    split(5)
                dve.wait_ge(s_sq, q + 1)
                dve.wait_ge(s_m, q + 1)
                dve.scalar_tensor_tensor(out=b_t[:], in0=yb[:], scalar=0.5, in1=i_t[:],
                                         op0=ALU.mult, op1=ALU.mult).then_inc(s_b, 1)
                dve.wait_ge(s_b, q + 1)
                if last:
                    dve.memset(a_t[:, HEAD:HEAD + GAP], 0.0)
                    dve.memset(b_t[:, HEAD:HEAD + GAP - 1], 0.0)
                    dve.tensor_copy(b_t[:, HEAD + GAP - 1:HEAD + GAP], col(HPREV)).then_inc(s_fix, 1)
                    dve.wait_ge(s_fix, j + 1)
                dve.wait_ge(s_carry, q + 1)
                dve.tensor_tensor_scan(yb[:, 0:n], a_t[:, 0:n], b_t[:, 0:n], h_carry[:], ALU.mult, ALU.add).then_inc(s_h, 1)
                dve.wait_ge(s_h, q + 1)
                if last:
                    dve.tensor_copy(st(SH_P, 1), yb[:, HEAD - 1:HEAD])
                    dve.tensor_copy(st(SH_S, 1), yb[:, EXT - 1:EXT]).then_inc(s_st, 1)
                    dve.memset(h_carry[:], 0.0).then_inc(s_carry, 1)
                else:
                    dve.tensor_copy(h_carry[:], yb[:, CHUNK - 1:CHUNK]).then_inc(s_carry, 1)
                dve.wait_ge(s_carry, q + 2)
                dve.wait_ge(s_gel, q + 1)
                for s, d, m in segs(last):
                    ins = dve.scalar_tensor_tensor(out=yb[:, d:d + m], in0=yb[:, d:d + m], scalar=0.5, in1=gel[:, s:s + m],
                                                   op0=ALU.mult, op1=ALU.mult)
                ins.then_inc(s_yb, 1)

            dve.memset(xc[:], 0.0)
            dve.memset(vb[:], 0.0)
            dve.memset(h_carry[:], 0.0).then_inc(s_carry, 1)
            dve.memset(u[:], 0.0).then_inc(s_hist, 1)
            dve.wait_ge(s_par, 16)
            lam = par[:, :, LAM]
            dve.scalar_tensor_tensor(out=sp_t[:, 0], in0=lam, scalar=-1.0, in1=lam, op0=ALU.mult, op1=ALU.max).then_inc(s_sp, 1)
            dve.wait_ge(s_spe, 1)
            dve.tensor_scalar(sp_t[:, 2], sp_t[:, 1], 2.0, None, ALU.add).then_inc(s_sp, 1)
            dve.wait_ge(s_sp, 2)
            dve.reciprocal(sp_t[:, 3], sp_t[:, 2]).then_inc(s_sp, 1)
            dve.wait_ge(s_sp, 3)
            dve.tensor_tensor(sp_t[:, 4], sp_t[:, 1], sp_t[:, 3], ALU.mult).then_inc(s_sp, 1)
            dve.wait_ge(s_sp, 4)
            dve.tensor_tensor(sp_t[:, 5], sp_t[:, 4], sp_t[:, 4], ALU.mult).then_inc(s_sp, 1)
            dve.wait_ge(s_sp, 5)
            dve.tensor_scalar(sp_t[:, 6], sp_t[:, 5], 1.0 / 15, None, ALU.mult).then_inc(s_sp, 1)
            for n, odd in enumerate((13, 11, 9, 7, 5, 3)):
                dve.wait_ge(s_sp, 6 + n)
                dve.scalar_tensor_tensor(out=sp_t[:, 6], in0=sp_t[:, 6], scalar=1.0 / odd, in1=sp_t[:, 5],
                                         op0=ALU.add, op1=ALU.mult).then_inc(s_sp, 1)
            dve.wait_ge(s_sp, 12)
            dve.scalar_tensor_tensor(out=sp_t[:, 6], in0=sp_t[:, 6], scalar=1.0, in1=sp_t[:, 4],
                                     op0=ALU.add, op1=ALU.mult)
            dve.tensor_scalar(sp_t[:, 7], lam, -1.0, 0.0, ALU.mult, ALU.max).then_inc(s_sp, 1)
            dve.wait_ge(s_sp, 13)
            dve.scalar_tensor_tensor(out=sp_t[:, 7], in0=sp_t[:, 6], scalar=2.0, in1=sp_t[:, 7],
                                     op0=ALU.mult, op1=ALU.add).then_inc(s_sp, 1)
            dve.wait_ge(s_sp, 14)
            dve.tensor_scalar(sp4[:], sp_t[:, 7], 4.0, None, ALU.mult)
            dve.tensor_scalar(nsp4[:], sp_t[:, 7], -4.0, None, ALU.mult)
            dve.tensor_scalar(hrb[:], par[:, :, RBIAS], 0.5, None, ALU.mult)
            dve.tensor_scalar(hib[:], par[:, :, IBIAS], 0.5, None, ALU.mult).then_inc(s_sp, 1)

            split_w(0, 0)
            for n in range(XP):
                split_x(0, n)
            for i in range(1, WP):
                split_w(0, i)
            for n in range(XP):
                split_x(1, n)
            step(0, 0, False, None)
            with dve.Fori(1, NCH - 1) as c:
                for n in range(XP):
                    split_x(c + 1, n)
                step(0, c, False, None)
            step(0, NCH - 1, True, lambda i: split_w(1, i))
            with dve.Fori(1, GROUPS - 1) as j:
                with dve.Fori(0, NCH - 1) as c:
                    step(j, c, False, None)
                step(j, NCH - 1, True, lambda i: split_w(j + 1, i))
            with dve.Fori(0, NCH - 1) as c:
                step(GROUPS - 1, c, False, None)
            step(GROUPS - 1, NCH - 1, True, None)


def tiles(eng, emit):
    emit(0, 0, 0)
    emit(1, 1, 0)
    with eng.Fori(1, NT // 2) as h:
        emit(h * 2, 0, h)
        emit(h * 2 + 1, 1, h)
    emit(NT - 1, 0, NT // 2)


def project_phase(nc, y_scr, x_rows, w_out, w_router, ln, consts_in, x1_scr, acc_scr, consts, ln_sb, logits):
    with ExitStack() as ctx:
        def sb(name, shape, dt=F32):
            return ctx.enter_context(nc.sbuf_tensor(name, shape, dt))

        def sem(name):
            return ctx.enter_context(nc.semaphore(name))

        wo_hi = sb("wo_hi", [P, KT, D], F32R)
        wo_lo = sb("wo_lo", [P, KT, D], F32R)
        wo_raw = sb("wo_raw", [P, 2, D])
        wr = sb("wr", [P, KT, NR])
        y_raw = sb("y_raw", [P, 2, KT, P])
        y_hi = sb("y_hi", [P, 2, KT, P], F32R)
        y_lo = sb("y_lo", [P, 2, KT, P], F32R)
        x_in = sb("x_in", [P, 2, D])
        s_sb = sb("s_sb", [P, 2, D])
        x1 = sb("x1_sb", [P, 2, D])
        ax1 = sb("ax1", [P, 2, D])
        x1_t = sb("x1_t", [P, 2, KT, P])
        zero = sb("zero", [P, D])
        stats = sb("stats", [P, 2, 2, 6])
        mv = sb("mv", [P, 2, 2])
        std = sb("std", [P, 2])
        rstd = sb("rstd", [P, 2])
        nmr = sb("nmr", [P, 2])
        eps = sb("eps", [P, 1])
        ps_m = [ctx.enter_context(nc.psum_tensor(f"ps_m{i}", [P, D], F32)) for i in range(2)]
        ps_t = ctx.enter_context(nc.psum_tensor("ps_t", [P, KT, P], F32))
        ps_l = ctx.enter_context(nc.psum_tensor("ps_l", [P, 512], F32))

        s_c = sem("s_const")
        s_wraw = [sem(f"s_woraw{i}") for i in range(2)]
        s_whi, s_wlo = sem("s_wohi"), sem("s_wolo")
        s_yraw = [sem(f"s_yraw{i}") for i in range(2)]
        s_yhi, s_ylo = sem("s_yhi"), sem("s_ylo")
        s_x = [sem(f"s_xin{i}") for i in range(2)]
        s_pad = sem("s_ypad")
        s_m = sem("s_pm")
        s_s = sem("s_s")
        s_bn, s_mv = sem("s_bn"), sem("s_mv")
        s_std, s_rstd, s_nmr = sem("s_std"), sem("s_rstd"), sem("s_nmr")
        s_xn, s_xg = sem("s_xn"), sem("s_xg")
        s_x1, s_ax = sem("s_x1"), sem("s_ax")
        s_x1o = [sem(f"s_x1o{i}") for i in range(2)]
        s_axo = [sem(f"s_axo{i}") for i in range(2)]
        s_tr, s_x1t = sem("s_tr"), sem("s_x1t")
        s_l, s_lo = sem("s_l"), sem("s_lev")
        s_z, s_zo = sem("s_zero"), sem("s_zo")
        block = ctx.enter_context(nc.Block())

        @block.gpsimd
        def _(pool):
            pool.dma_start(consts[:], consts_in).then_inc(s_c, 16)
            pool.dma_start(ln_sb[:], ln).then_inc(s_c, 16)
            pool.dma_start(wr[:], w_router).then_inc(s_c, 16)
            pool.wait_ge(s_c, 48)
            pool.memset(zero[:], 0.0).then_inc(s_z, 1)
            pool.wait_ge(s_z, 1)
            pool.dma_start(x1_scr[ROWS:ROWS + P, :], zero[:]).then_inc(s_zo, 16)
            pool.dma_start(acc_scr[ROWS:ROWS + P, :], zero[:]).then_inc(s_zo, 16)

            def tile(t, par, h):
                pool.wait_ge(s_xg, t + 1)
                if not (isinstance(t, int) and t < 2):
                    pool.wait_ge(s_x1o[par], h * 16)
                    pool.wait_ge(s_tr, t - 1)
                    pool.wait_ge(s_ax, t - 1)
                pool.tensor_tensor(x1[:, par], s_sb[:, par], ln_sb[:, 1], ALU.add).then_inc(s_x1, 1)
            tiles(pool, tile)
            pool.wait_ge(s_zo, 32)

        @block.sync
        def _(sp):
            def load_w(k):
                if k >= 2:
                    sp.wait_ge(s_wlo, k - 1)
                sp.dma_start(wo_raw[:, k % 2], w_out[:, k]).then_inc(s_wraw[k % 2], 16)

            def load(t, par, h, tail=False):
                n = TAIL if tail else P
                if not (isinstance(t, int) and t < 2):
                    sp.wait_ge(s_s, t - 1)
                    sp.wait_ge(s_ylo, t - 1)
                if tail:
                    sp.wait_ge(s_pad, 1)
                sp.dma_start(y_raw[:, par, :, 0:n],
                             y_scr[:, :, bass.ds(t * P, n)].rearrange("k p t -> p k t")).then_inc(s_yraw[par], 16)
                sp.dma_start(x_in[:, par], x_rows[bass.ds(t * P, P), :]).then_inc(s_x[par], 16)

            load(0, 0, 0)
            load_w(0)
            load_w(1)
            load(1, 1, 0)
            for k in range(2, KT):
                load_w(k)
            with sp.Fori(0, NT // 2 - 1) as h:
                for par in range(2):
                    load(h * 2 + (par + 2), par, h + 1)
            load(NT - 1, 0, NT // 2, tail=True)
            for par in range(2):
                sp.wait_ge(s_x1o[par], 16 * (NT // 2 + 1 - par))
                sp.wait_ge(s_axo[par], 16 * (NT // 2 + 1 - par))

        @block.tensor
        def _(pe):
            def project(t, par, h):
                pe.wait_ge(s_ylo, t + 1)
                if not (isinstance(t, int) and t < 2):
                    pe.wait_ge(s_s, t - 1)
                for k in range(KT):
                    if isinstance(t, int) and t == 0:
                        pe.wait_ge(s_wlo, k + 1)
                    for n, (y, w) in enumerate(((y_hi, wo_hi), (y_hi, wo_lo), (y_lo, wo_hi))):
                        for f in range(2):
                            mm = pe.matmul(ps_m[par][:, f * 512:f * 512 + 512], y[:, par, k], w[:, k, f * 512:f * 512 + 512],
                                           start=(k == 0 and n == 0), stop=(k == KT - 1 and n == 2))
                mm.then_inc(s_m, 1)

            def turn(t, par):
                pe.wait_ge(s_x1, t + 1)
                pe.wait_ge(s_x1t, t)
                for k in range(KT):
                    mm = pe.transpose(ps_t[:, k], x1[:, par, k * P:(k + 1) * P], consts[:, C_ID:C_ID + P])
                mm.then_inc(s_tr, 1)

            def route(t, par):
                pe.wait_ge(s_x1t, t + 1)
                pe.wait_ge(s_lo, t + 1)
                for k in range(KT):
                    mm = pe.matmul(ps_l[:, 0:NR], x1_t[:, par, k], wr[:, k], start=(k == 0), stop=(k == KT - 1))
                mm.then_inc(s_l, 1)

            pe.wait_ge(s_c, 48)
            def tile(t, par, h):
                project(t, par, h)
                if not (isinstance(t, int) and t < 2):
                    route(t - 2, par)
                if not (isinstance(t, int) and t < 1):
                    turn(t - 1, 1 - par)
            tiles(pe, tile)
            route(NT - 2, (NT - 2) % 2)
            turn(NT - 1, (NT - 1) % 2)
            route(NT - 1, (NT - 1) % 2)

        @block.scalar
        def _(act):
            def split_y(t, par, h):
                act.wait_ge(s_yraw[par], h * 16 + 16)
                if not (isinstance(t, int) and t < 2):
                    act.wait_ge(s_m, t - 1)
                act.activation(y_hi[:, par], y_raw[:, par], ACT.Copy).then_inc(s_yhi, 1)

            def turned(t, par):
                act.wait_ge(s_tr, t + 1)
                if not (isinstance(t, int) and t < 2):
                    act.wait_ge(s_lo, t)
                act.activation(x1_t[:, par], ps_t[:], ACT.Copy).then_inc(s_x1t, 1)

            def store_ax(t, par):
                act.wait_ge(s_ax, t + 1)
                act.dma_start(acc_scr[bass.ds(t * P, P), :], ax1[:, par]).then_inc(s_axo[par], 16)

            def tile(t, par, h, more=True):
                if more:
                    split_y(t + 2, par, h + 1)
                if not (isinstance(t, int) and t < 1):
                    store_ax(t - 1, 1 - par)
                    turned(t - 1, 1 - par)
                act.wait_ge(s_mv, t + 1)
                act.activation(std[:, par:par + 1], mv[:, par, 1:2], ACT.Sqrt, bias=eps[:]).then_inc(s_std, 1)
                act.wait_ge(s_nmr, t + 1)
                act.activation(s_sb[:, par], s_sb[:, par], ACT.Identity, scale=rstd[:, par:par + 1],
                               bias=nmr[:, par:par + 1]).then_inc(s_xn, 1)
                act.wait_ge(s_x1, t + 1)
                act.dma_start(x1_scr[bass.ds(t * P, P), :], x1[:, par]).then_inc(s_x1o[par], 16)
                if not (isinstance(t, int) and t < 2):
                    act.wait_ge(s_axo[par], h * 16)
                act.activation(ax1[:, par], x1[:, par], ACT.Copy, scale=ALPHA).then_inc(s_ax, 1)

            split_y(0, 0, 0)
            for k in range(KT):
                act.wait_ge(s_wraw[k % 2], 16 * (k // 2 + 1))
                act.activation(wo_hi[:, k], wo_raw[:, k % 2], ACT.Copy).then_inc(s_whi, 1)
                if k == 1:
                    split_y(1, 1, 0)
            tile(0, 0, 0)
            tile(1, 1, 0)
            with act.Fori(1, NT // 2 - 1) as h:
                tile(h * 2, 0, h)
                tile(h * 2 + 1, 1, h)
            tile(NT - 3, 0, NT // 2 - 1)
            tile(NT - 2, 1, NT // 2 - 1, more=False)
            tile(NT - 1, 0, NT // 2, more=False)
            store_ax(NT - 1, 0)
            turned(NT - 1, 0)

        @block.vector
        def _(dve):
            def split_y(t, par):
                dve.wait_ge(s_yhi, t + 1)
                dve.tensor_tensor(y_lo[:, par], y_raw[:, par], y_hi[:, par].bitcast(F32), ALU.subtract).then_inc(s_ylo, 1)

            def logits_out(t):
                dve.wait_ge(s_l, t + 1)
                dve.tensor_copy(logits[:, bass.ds(t, 1)].rearrange("p o n -> p (o n)"), ps_l[:, 0:NR]).then_inc(s_lo, 1)

            def tile(t, par, h, more=True, pad=False):
                dve.wait_ge(s_m, t + 1)
                dve.wait_ge(s_x[par], h * 16 + 16)
                if not (isinstance(t, int) and t < 2):
                    dve.wait_ge(s_x1, t - 1)
                for f in range(2):
                    c = slice(f * 512, f * 512 + 512)
                    ins = dve.scalar_tensor_tensor(out=s_sb[:, par, c], in0=x_in[:, par, c], scalar=ALPHA,
                                                   in1=ps_m[par][:, c], op0=ALU.mult, op1=ALU.add)
                ins.then_inc(s_s, 1)
                dve.wait_ge(s_s, t + 1)
                for f in range(2):
                    ins = dve.bn_stats(stats[:, par, f], s_sb[:, par, f * 512:f * 512 + 512])
                ins.then_inc(s_bn, 1)
                dve.wait_ge(s_bn, 1)
                dve.wait_ge(s_bn, t + 1)
                dve.bn_aggr(mv[:, par], stats[:, par]).then_inc(s_mv, 1)
                if pad:
                    dve.wait_ge(s_ylo, NT - 2)
                    dve.memset(y_raw[:, 0], 0.0).then_inc(s_pad, 1)
                if more:
                    split_y(t + 2, par)
                dve.wait_ge(s_std, t + 1)
                dve.reciprocal(rstd[:, par:par + 1], std[:, par:par + 1]).then_inc(s_rstd, 1)
                dve.wait_ge(s_rstd, t + 1)
                dve.scalar_tensor_tensor(out=nmr[:, par:par + 1], in0=mv[:, par, 0:1], scalar=-1.0,
                                         in1=rstd[:, par:par + 1], op0=ALU.mult, op1=ALU.mult).then_inc(s_nmr, 1)
                dve.wait_ge(s_xn, t + 1)
                dve.tensor_tensor(s_sb[:, par], s_sb[:, par], ln_sb[:, 0], ALU.mult).then_inc(s_xg, 1)
                if not (isinstance(t, int) and t < 2):
                    logits_out(t - 2)

            dve.memset(eps[:], LN_EPS).then_inc(s_lo, 1)
            dve.wait_ge(s_c, 48)
            split_y(0, 0)
            for k in range(KT):
                dve.wait_ge(s_whi, k + 1)
                dve.tensor_tensor(wo_lo[:, k], wo_raw[:, k % 2], wo_hi[:, k].bitcast(F32), ALU.subtract).then_inc(s_wlo, 1)
                if k == 1:
                    split_y(1, 1)
            tile(0, 0, 0)
            tile(1, 1, 0)
            with dve.Fori(1, NT // 2 - 1) as h:
                tile(h * 2, 0, h)
                tile(h * 2 + 1, 1, h)
            tile(NT - 3, 0, NT // 2 - 1, pad=True)
            tile(NT - 2, 1, NT // 2 - 1, more=False)
            tile(NT - 1, 0, NT // 2, more=False)
            logits_out(NT - 2)
            logits_out(NT - 1)


def route_phase(nc, consts, logits, ids, gates, plan):
    with ExitStack() as ctx:
        def sb(name, shape, dt=F32):
            return ctx.enter_context(nc.sbuf_tensor(name, shape, dt))

        def sem(name):
            return ctx.enter_context(nc.semaphore(name))

        t3 = [sb(f"t3_{i}", [P, NT, NG]) for i in range(4)]
        lg, q4, goh, e4 = t3
        e4b = sb("e4b", [P, NT, NE_G])
        oh = [sb(f"oh{i}", [P, NT, NE_G]) for i in range(2)]
        col = sb("col", [P, 10, NT])
        gmax, gsum, ggate, mx, m1, m2, ex, rec = (col[:, i] for i in range(8))
        wts = sb("wts", [P, TOPK, NT])
        a16 = [sb(f"a16_{i}", [P, NT, NG, NE_G]) for i in range(3)]
        big = sb("big", [P, NT, NG, NE_G])
        tot = sb("tot", [P, NE, NT])
        inc = sb("inc", [P, NE, NT])
        slot = sb("slot", [P, NT, NE])
        cmpc = sb("cmpc", [P, NE, NT])
        ecol = sb("ecol", [P, 4, NE])
        ntile, ecum, base = (ecol[:, i] for i in range(3))
        sl = sb("sl", [P, TOPK, NT])
        sli = sb("sli", [P, TOPK, NT], I32)
        shi_i = sb("shi_i", [P, TOPK, NT], I32)
        slo_i = sb("slo_i", [P, TOPK, NT], I32)
        shi = sb("shi", [P, TOPK, NT])
        slo = sb("slo", [P, TOPK, NT])
        at_lo = sb("at_lo", [P, TOPK, P])
        at_hi = sb("at_hi", [P, TOPK, 2, STEPS])
        tab = sb("tab", [P, STEPS])
        cmps = sb("cmps", [1, STEPS, NE - 1])
        est = sb("est", [1, STEPS + 1])
        new = sb("new", [1, STEPS])
        pairs = sb("pairs", [1, 1], I32)
        ps_pos = ctx.enter_context(nc.psum_tensor("ps_pos", [P, 512], F32))
        ps_tot = ctx.enter_context(nc.psum_tensor("ps_tot", [P, 512], F32))
        ps_tab = ctx.enter_context(nc.psum_tensor("ps_tab", [P, 512], F32))

        s_dve = sem("s_rdve")
        s_dif = sem("s_rdif")
        s_exp = sem("s_rexp")
        s_m2 = sem("s_rm2")
        s_asg = sem("s_rasg")
        s_cnt = sem("s_rcnt")
        s_hot = sem("s_rhot")
        s_put = sem("s_rput")
        block = ctx.enter_context(nc.Block())
        count = [0]

        @block.scalar
        def _(act):
            act.wait_ge(s_dif, 1)
            act.activation(q4[:], lg[:], ACT.Exp).then_inc(s_exp, 1)
            act.wait_ge(s_m2, 1)
            act.activation(ex, m2, ACT.Exp).then_inc(s_exp, 1)

        @block.tensor
        def _(pe):
            a = a16[2][:].rearrange("p t g e -> p (t g e)")
            pe.wait_ge(s_asg, 1)
            pe.matmul(ps_pos[:, 0:NT * NE], consts[:, C_TRI:C_TRI + P], a, start=True, stop=True)
            pe.matmul(ps_tot[:, 0:NT * NE], consts[:, C_ONE:C_ONE + P], a, start=True, stop=True).then_inc(s_cnt, 1)

            def put(t, first, last):
                for c in range(TOPK):
                    pe.wait_ge(s_hot, t * TOPK + (c + 1))
                    pe.matmul(ps_tab[:, 0:2 * STEPS], at_lo[:, c], at_hi[:, c].rearrange("p a s -> p (a s)"),
                              start=(first and c == 0), stop=(last and c == 1)).then_inc(s_put, 1)
            put(0, True, False)
            with pe.Fori(1, NT - 1) as t:
                put(t, False, False)
            put(NT - 1, False, True)

        @block.vector
        def _(dve):
            def then(ins):
                count[0] += 1
                ins.then_inc(s_dve, 1)
                dve.wait_ge(s_dve, count[0])

            def bc(ap, n):
                return ap.unsqueeze(2).broadcast_to((P, NT, n))

            dec = consts[:, C_DEC:C_DEC + NG].unsqueeze(1).broadcast_to((P, NT, NG))

            def first_max(out, diff):
                then(dve.scalar_tensor_tensor(out=q4[:], in0=diff, scalar=0.0, in1=dec, op0=ALU.is_ge, op1=ALU.mult))
                then(dve.tensor_reduce(mx, q4[:], AX.X, ALU.max))
                then(dve.tensor_tensor(out, q4[:], bc(mx, NG), ALU.is_equal))

            then(dve.tensor_reduce(gmax, logits[:, :, 0:NG], AX.X, ALU.max))
            dve.tensor_tensor(lg[:], logits[:, :, 0:NG], bc(gmax, NG), ALU.subtract).then_inc(s_dif, 1)
            dve.wait_ge(s_exp, 1)
            then(dve.tensor_reduce(gsum, q4[:], AX.X, ALU.add))
            then(dve.reciprocal(ggate, gsum))
            first_max(goh[:], lg[:])
            le = logits[:, :, NG:NR].rearrange("p t (g e) -> p t g e", g=NG)
            goh_b = goh[:].unsqueeze(3).broadcast_to((P, NT, NG, NE_G))
            then(dve.tensor_tensor(big[:], le, goh_b, ALU.mult))
            then(dve.tensor_reduce(e4[:], big[:].rearrange("p t g e -> p t e g"), AX.X, ALU.add))
            then(dve.tensor_reduce(m1, e4[:], AX.X, ALU.max))
            then(dve.tensor_tensor(e4[:], e4[:], bc(m1, NE_G), ALU.subtract))
            first_max(oh[0][:], e4[:])
            then(dve.scalar_tensor_tensor(out=e4b[:], in0=oh[0][:], scalar=-1e30, in1=e4[:], op0=ALU.mult, op1=ALU.add))
            dve.tensor_reduce(m2, e4b[:], AX.X, ALU.max).then_inc(s_m2, 1)
            dve.wait_ge(s_m2, 1)
            then(dve.tensor_tensor(e4b[:], e4b[:], bc(m2, NE_G), ALU.subtract))
            first_max(oh[1][:], e4b[:])
            dve.wait_ge(s_exp, 2)
            then(dve.tensor_scalar(gsum, ex, 1.0, None, ALU.add))
            then(dve.reciprocal(rec, gsum))
            then(dve.tensor_tensor(wts[:, 0], rec, ggate, ALU.mult))
            then(dve.tensor_tensor(wts[:, 1], wts[:, 0], ex, ALU.mult))
            then(dve.tensor_tensor(goh[:], goh[:], bc(consts[:, C_VAL:C_VAL + NT], NG), ALU.mult))
            for c in range(TOPK):
                then(dve.tensor_tensor(a16[c][:], goh_b, oh[c][:].unsqueeze(2).broadcast_to((P, NT, NG, NE_G)), ALU.mult))
            dve.tensor_tensor(a16[2][:], a16[0][:], a16[1][:], ALU.add).then_inc(s_asg, 1)
            dve.wait_ge(s_cnt, 1)
            then(dve.tensor_copy(tot[:], ps_tot[:, 0:NT * NE].rearrange("p (t e) -> p e t", e=NE)))
            flat = lambda x: x[:].rearrange("p e t -> p (e t)")
            then(dve.tensor_tensor_scan(flat(inc), consts[:, C_SEG:C_SEG + NT * NE], flat(tot), 0.0, ALU.mult, ALU.add))
            then(dve.tensor_tensor(tot[:], inc[:], tot[:], ALU.subtract))
            then(dve.tensor_tensor(cmpc[:], inc[:, :, NT - 1].unsqueeze(2).broadcast_to((P, NE, NT)),
                                   consts[:, C_THR:C_THR + NT].unsqueeze(1).broadcast_to((P, NE, NT)), ALU.is_gt))
            then(dve.tensor_reduce(ntile, cmpc[:], AX.X, ALU.add))
            then(dve.tensor_scalar(ntile, ntile, 1.0, None, ALU.max))
            then(dve.tensor_tensor_scan(ecum, consts[:, C_ONE:C_ONE + NE], ntile, 0.0, ALU.mult, ALU.add))
            then(dve.tensor_tensor(base, ecum, ntile, ALU.subtract))
            then(dve.tensor_scalar(base, base, float(P), None, ALU.mult))
            then(dve.tensor_tensor(slot[:], tot[:].rearrange("p e t -> p t e"),
                                   ps_pos[:, 0:NT * NE].rearrange("p (t e) -> p t e", e=NE), ALU.add))
            then(dve.tensor_tensor(slot[:], slot[:], base.unsqueeze(1).broadcast_to((P, NT, NE)), ALU.add))
            for c in range(TOPK):
                then(dve.tensor_tensor(big[:], a16[c][:], slot[:].rearrange("p t (g e) -> p t g e", g=NG), ALU.mult))
                then(dve.tensor_reduce(sl[:, c], big[:].rearrange("p t g e -> p t (g e)"), AX.X, ALU.add))
                then(dve.tensor_tensor(sl[:, c], sl[:, c], consts[:, C_INV:C_INV + NT], ALU.add))
            then(dve.tensor_copy(sli[:], sl[:]))
            dve.tensor_scalar(shi_i[:], sli[:], 7, None, ALU.logical_shift_right)
            then(dve.tensor_scalar(slo_i[:], sli[:], P - 1, None, ALU.bitwise_and))
            dve.tensor_copy(shi[:], shi_i[:])
            then(dve.tensor_copy(slo[:], slo_i[:]))

            def put(t, first):
                one = lambda ap: ap[:, bass.ds(t, 1)]
                for c in range(TOPK):
                    if not first:
                        dve.wait_ge(s_put, t * TOPK + (c - 1))
                    dve.tensor_scalar(at_lo[:, c], consts[:, C_IO:C_IO + P], one(slo[:, c]), None, ALU.is_equal)
                    dve.tensor_scalar(at_hi[:, c, 0], consts[:, C_IO:C_IO + STEPS], one(shi[:, c]),
                                      one(consts[:, C_TOK:C_TOK + NT]), ALU.is_equal, ALU.mult)
                    dve.tensor_scalar(at_hi[:, c, 1], consts[:, C_IO:C_IO + STEPS], one(shi[:, c]),
                                      one(wts[:, c]), ALU.is_equal, ALU.mult).then_inc(s_hot, 1)
            put(0, True)
            with dve.Fori(1, NT) as t:
                put(t, False)
            then(dve.tensor_tensor(cmps[:], consts[0:1, C_IO:C_IO + STEPS].unsqueeze(2).broadcast_to((1, STEPS, NE - 1)),
                                   ecum[0:1, 0:NE - 1].unsqueeze(1).broadcast_to((1, STEPS, NE - 1)), ALU.is_ge))
            dve.memset(est[:, 0:1], -1.0)
            then(dve.tensor_reduce(est[:, 1:], cmps[:], AX.X, ALU.add))
            dve.tensor_copy(plan[:, 0], est[:, 1:])
            then(dve.tensor_scalar(pairs[:], ecum[0:1, NE - 1:NE], float(1 - NE), None, ALU.add))
            dve.tensor_scalar(plan[:, 2, 0:1], pairs[:], 1, None, ALU.logical_shift_right)
            then(dve.tensor_tensor(new[:], est[:, 1:], est[:, 0:STEPS], ALU.not_equal))
            dve.scalar_tensor_tensor(out=plan[:, 1], in0=est[:, 1:], scalar=float(NE - 1), in1=new[:],
                                     op0=ALU.is_lt, op1=ALU.mult)
            dve.wait_ge(s_put, NT * TOPK)
            then(dve.tensor_scalar(tab[:], ps_tab[:, 0:STEPS], 0.0, consts[:, C_PAD:C_PAD + 1], ALU.is_equal, ALU.mult))
            dve.scalar_tensor_tensor(out=ids[:], in0=ps_tab[:, 0:STEPS], scalar=-1.0, in1=tab[:], op0=ALU.add, op1=ALU.add)
            then(dve.tensor_copy(gates[:], ps_tab[:, STEPS:2 * STEPS]))


def experts_phase(nc, x1_scr, acc_scr, w13, w2, consts, ids, gates, plan):
    with ExitStack() as ctx:
        def sb(name, shape, dt=F32):
            return ctx.enter_context(nc.sbuf_tensor(name, shape, dt))

        def sem(name):
            return ctx.enter_context(nc.semaphore(name))

        w13_raw = sb("w13_raw", [P, KT, 2 * FE])
        w2_raw = sb("w2_raw", [P, FT, D])
        w13_hi = sb("w13_hi", [P, 2, KT, 2 * FE], F32R)
        w13_lo = sb("w13_lo", [P, 2, KT, 2 * FE], F32R)
        w2_hi = sb("w2_hi", [P, 2, FT, D], F32R)
        w2_lo = sb("w2_lo", [P, 2, FT, D], F32R)
        xg = sb("xg", [P, 2, D])
        xt_hi = sb("xt_hi", [P, 2, KT, P], F32R)
        xt_lo = sb("xt_lo", [P, 2, KT, P], F32R)
        sil = sb("sil", [P, FE])
        hid = sb("hid", [P, FE])
        ht_hi = sb("ht_hi", [P, FT, P], F32R)
        ht_lo = sb("ht_lo", [P, FT, P], F32R)
        out = sb("out_sb", [P, 2, D])
        id_g = sb("id_g", [P, 2], I32)
        id_s = sb("id_s", [P, 2], I32)
        ps_x = ctx.enter_context(nc.psum_tensor("ps_x", [P, KT, P], F32))
        ps_h = [ctx.enter_context(nc.psum_tensor(f"ps_h{i}", [P, 2 * FE], F32)) for i in range(2)]
        ps_ht = ctx.enter_context(nc.psum_tensor("ps_ht", [P, 4, P], F32))
        ps_o = [ctx.enter_context(nc.psum_tensor(f"ps_o{i}", [P, 512], F32)) for i in range(2)]

        s_r13, s_r2 = sem("s_r13"), sem("s_r2")
        s_13hi, s_13lo = sem("s_13hi"), sem("s_13lo")
        s_2hi, s_2lo = sem("s_2hi"), sem("s_2lo")
        s_id0, s_idg = sem("s_id0"), sem("s_idg")
        s_ids = sem("s_ids")
        s_xg = [sem(f"s_xg{i}") for i in range(2)]
        s_tx, s_xhi, s_xlo = sem("s_tx"), sem("s_xthi"), sem("s_xtlo")
        s_h, s_sil, s_hid = sem("s_hm"), sem("s_sil"), sem("s_hid")
        s_th, s_hhi, s_hlo = sem("s_th"), sem("s_hthi"), sem("s_htlo")
        s_o, s_oa, s_ov = sem("s_o"), sem("s_oa"), sem("s_ov")
        s_add = sem("s_add")
        block = ctx.enter_context(nc.Block())

        def steps(eng, emit):
            pairs = eng.value_load(plan[0:1, 2, 0:1], min_val=0, max_val=(STEPS - NE) // 2) + NE // 2
            emit(0, 0, 0, 2)
            emit(1, 1, 0, 2)
            with eng.Fori(1, STEPS // 2 - 1) as h:
                with eng.If(h < pairs - 1):
                    emit(h * 2, 0, h, 2)
                    emit(h * 2 + 1, 1, h, 2)
            emit(pairs * 2 - 2, 0, pairs - 1, 1)
            emit(pairs * 2 - 1, 1, pairs - 1, 0)
            return pairs * 2 - 1

        def early(s, n):
            return isinstance(s, int) and s < n

        @block.sync
        def _(sp):
            sp.dma_start(w13_raw[:], w13[0]).then_inc(s_r13, 16)
            sp.dma_start(w2_raw[:], w2[0]).then_inc(s_r2, 16)
            with sp.Fori(1, NE) as e:
                sp.wait_ge(s_13lo, e * 2)
                sp.dma_start(w13_raw[:], w13[bass.ds(e, 1)].rearrange("o p k n -> p (o k) n")).then_inc(s_r13, 16)
                sp.wait_ge(s_2lo, e)
                sp.dma_start(w2_raw[:], w2[bass.ds(e, 1)].rearrange("o p k n -> p (o k) n")).then_inc(s_r2, 16)

        @block.gpsimd
        def _(pool):
            def gather(s, par, h):
                if not early(s, 2):
                    pool.wait_ge(s_tx, s - 1)
                if early(s, 2):
                    pool.tensor_copy(id_g[:, par:par + 1], ids[:, s:s + 1]).then_inc(s_id0, 1)
                    pool.wait_ge(s_id0, s + 1)
                else:
                    pool.tensor_copy(id_g[:, par:par + 1], ids[:, bass.ds(s, 1)]).then_inc(s_idg, 1)
                    pool.wait_ge(s_idg, 1)
                    pool.wait_ge(s_idg, s - 1)
                pool.indirect_dma_start(xg[:, par], None, x1_scr,
                                        bass.IndirectOffsetOnAxis(id_g[:, par:par + 1], 0)).then_inc(s_xg[par], 16)

            def add(s, par):
                pool.wait_ge(s_add, s * 16)
                done = s + 1
                pool.wait_ge(s_oa, done)
                pool.tensor_copy(id_s[:, par:par + 1], ids[:, bass.ds(s, 1)]).then_inc(s_ids, 1)
                pool.wait_ge(s_ids, 1)
                pool.wait_ge(s_ids, done)
                pool.wait_ge(s_ov, done)
                pool.indirect_dma_start(acc_scr, bass.IndirectOffsetOnAxis(id_s[:, par:par + 1], 0),
                                        out[:, par], None, compute_op=ALU.add).then_inc(s_add, 16)

            def step(s, par, h, left):
                if left == 2:
                    gather(s + 2, par, h + 1)
                if not early(s, 1):
                    add(s - 1, 1 - par)

            gather(0, 0, 0)
            gather(1, 1, 0)
            last = steps(pool, step)
            add(last, 1)
            pool.wait_ge(s_add, last * 16 + 16)

        @block.tensor
        def _(pe):
            def turn(s, par, h):
                pe.wait_ge(s_xg[par], h * 16 + 16)
                pe.wait_ge(s_xlo, s)
                for k in range(KT):
                    mm = pe.transpose(ps_x[:, k], xg[:, par, k * P:(k + 1) * P], consts[:, C_ID:C_ID + P])
                mm.then_inc(s_tx, 1)

            def output(s, expert):
                at = expert % 2
                pe.wait_ge(s_hlo, s + 1)
                pe.wait_ge(s_2lo, expert + 1)
                pe.wait_ge(s_oa, s)
                pe.wait_ge(s_ov, s)
                for k in range(FT):
                    for n, (x, w) in enumerate(((ht_hi, w2_hi), (ht_hi, w2_lo), (ht_lo, w2_hi))):
                        for f in range(2):
                            mm = pe.matmul(ps_o[f][:], x[:, k],
                                           w[:, bass.ds(at, 1), k, f * 512:f * 512 + 512].rearrange("p o n -> p (o n)"),
                                           start=(k == 0 and n == 0), stop=(k == FT - 1 and n == 2))
                mm.then_inc(s_o, 1)

            def step(s, par, h, left):
                expert = pe.value_load(plan[0:1, 0, bass.ds(s, 1)], min_val=0, max_val=NE - 1)
                at = expert % 2
                if left:
                    turn(s + 1, 1 - par, h if par == 0 else h + 1)
                pe.wait_ge(s_xlo, s + 1)
                pe.wait_ge(s_13lo, expert * 2 + 2)
                if not early(s, 2):
                    pe.wait_ge(s_hid, s - 1)
                for k in range(KT):
                    for n, (x, w) in enumerate(((xt_hi, w13_hi), (xt_hi, w13_lo), (xt_lo, w13_hi))):
                        mm = pe.matmul(ps_h[par][:], x[:, par, k], w[:, bass.ds(at, 1), k].rearrange("p o n -> p (o n)"),
                                       start=(k == 0 and n == 0), stop=(k == KT - 1 and n == 2))
                mm.then_inc(s_h, 1)
                if not early(s, 1):
                    output(s - 1, pe.value_load(plan[0:1, 0, bass.ds(s - 1, 1)], min_val=0, max_val=NE - 1))
                pe.wait_ge(s_hid, s + 1)
                for k in range(FT):
                    mm = pe.transpose(ps_ht[:, k], hid[:, k * P:(k + 1) * P], consts[:, C_ID:C_ID + P])
                mm.then_inc(s_th, 1)

            turn(0, 0, 0)
            last = steps(pe, step)
            output(last, pe.value_load(plan[0:1, 0, bass.ds(last, 1)], min_val=0, max_val=NE - 1))

        HK = KT // 2

        @block.scalar
        def _(act):
            def split13(n, at):
                act.wait_ge(s_r13, n * 16 + 16)
                for i in range(2):
                    act.activation(w13_hi[:, at, i * HK:i * HK + HK].rearrange("p o k n -> p (o k) n"),
                                   w13_raw[:, i * HK:i * HK + HK], ACT.Copy).then_inc(s_13hi, 1)

            def split2(n, at):
                act.wait_ge(s_r2, n * 16 + 16)
                act.activation(w2_hi[:, at].rearrange("p o k n -> p (o k) n"), w2_raw[:], ACT.Copy).then_inc(s_2hi, 1)

            def h_hi(s):
                act.wait_ge(s_th, s + 1)
                act.activation(ht_hi[:], ps_ht[:, 0:FT], ACT.Copy).then_inc(s_hhi, 1)

            def x_hi(s, par):
                act.wait_ge(s_tx, s + 1)
                if not early(s, 2):
                    act.wait_ge(s_h, s - 1)
                act.activation(xt_hi[:, par], ps_x[:], ACT.Copy).then_inc(s_xhi, 1)

            def out_half(s, par):
                act.wait_ge(s_o, s + 1)
                if not early(s, 1):
                    act.wait_ge(s_ids, s)
                act.activation(out[:, par, 0:512], ps_o[0][:], ACT.Copy).then_inc(s_oa, 1)

            def step(s, par, h, left):
                expert = act.value_load(plan[0:1, 0, bass.ds(s, 1)], min_val=0, max_val=NE - 1)
                split = act.value_load(plan[0:1, 1, bass.ds(s, 1)], min_val=0, max_val=1)
                at = bass.ds((expert + 1) % 2, 1)
                if not early(s, 1):
                    h_hi(s - 1)
                if left:
                    x_hi(s + 1, 1 - par)
                with act.If(split):
                    split13(expert + 1, at)
                act.wait_ge(s_h, s + 1)
                act.wait_ge(s_hid, s)
                act.activation(sil[:], ps_h[par][:, 0:FE], ACT.Silu).then_inc(s_sil, 1)
                if not early(s, 1):
                    out_half(s - 1, 1 - par)
                with act.If(split):
                    split2(expert + 1, at)
                act.wait_ge(s_sil, 1)
                act.wait_ge(s_sil, s + 1)

            split13(0, bass.ds(0, 1))
            split2(0, bass.ds(0, 1))
            x_hi(0, 0)
            last = steps(act, step)
            h_hi(last)
            out_half(last, 1)

        @block.vector
        def _(dve):
            def split13(n, at):
                for i in range(2):
                    dve.wait_ge(s_13hi, n * 2 + (i + 1))
                    rows = slice(i * HK, i * HK + HK)
                    dve.tensor_tensor(w13_lo[:, at, rows].rearrange("p o k n -> p (o k) n"), w13_raw[:, rows],
                                      w13_hi[:, at, rows].rearrange("p o k n -> p (o k) n").bitcast(F32),
                                      ALU.subtract).then_inc(s_13lo, 1)

            def split2(n, at):
                dve.wait_ge(s_2hi, n + 1)
                dve.tensor_tensor(w2_lo[:, at].rearrange("p o k n -> p (o k) n"), w2_raw[:],
                                  w2_hi[:, at].rearrange("p o k n -> p (o k) n").bitcast(F32),
                                  ALU.subtract).then_inc(s_2lo, 1)

            def h_lo(s):
                dve.wait_ge(s_hhi, s + 1)
                dve.tensor_tensor(ht_lo[:], ps_ht[:, 0:FT], ht_hi[:].bitcast(F32), ALU.subtract).then_inc(s_hlo, 1)

            def x_lo(s, par):
                dve.wait_ge(s_xhi, s + 1)
                dve.tensor_tensor(xt_lo[:, par], ps_x[:], xt_hi[:, par].bitcast(F32), ALU.subtract).then_inc(s_xlo, 1)

            def out_half(s, par):
                dve.wait_ge(s_o, s + 1)
                if not early(s, 1):
                    dve.wait_ge(s_ids, s)
                dve.tensor_copy(out[:, par, 512:D], ps_o[1][:]).then_inc(s_ov, 1)

            def step(s, par, h, left):
                expert = dve.value_load(plan[0:1, 0, bass.ds(s, 1)], min_val=0, max_val=NE - 1)
                split = dve.value_load(plan[0:1, 1, bass.ds(s, 1)], min_val=0, max_val=1)
                at = bass.ds((expert + 1) % 2, 1)
                if not early(s, 1):
                    h_lo(s - 1)
                if left:
                    x_lo(s + 1, 1 - par)
                with dve.If(split):
                    split13(expert + 1, at)
                dve.wait_ge(s_sil, s + 1)
                dve.wait_ge(s_th, s)
                dve.scalar_tensor_tensor(out=hid[:], in0=sil[:], scalar=gates[:, bass.ds(s, 1)],
                                         in1=ps_h[par][:, FE:2 * FE], op0=ALU.mult, op1=ALU.mult).then_inc(s_hid, 1)
                if not early(s, 1):
                    out_half(s - 1, 1 - par)
                with dve.If(split):
                    split2(expert + 1, at)
                dve.wait_ge(s_hid, 1)
                dve.wait_ge(s_hid, s + 1)

            split13(0, bass.ds(0, 1))
            split2(0, bass.ds(0, 1))
            x_lo(0, 0)
            last = steps(dve, step)
            h_lo(last)
            out_half(last, 1)


def finish_phase(nc, acc_scr, y_out, ln_sb):
    with ExitStack() as ctx:
        def sb(name, shape, dt=F32):
            return ctx.enter_context(nc.sbuf_tensor(name, shape, dt))

        def sem(name):
            return ctx.enter_context(nc.semaphore(name))

        v = sb("v", [P, NT, D])
        stats = sb("stats2", [P, NT, 2, 6])
        mv = sb("mv2", [P, NT, 2])
        std = sb("std2", [P, NT])
        rstd = sb("rstd2", [P, NT])
        nmr = sb("nmr2", [P, NT])
        eps = sb("eps2", [P, 1])
        s_in = [sem(f"s_fin{i}") for i in range(NT)]
        s_eps = sem("s_eps2")
        s_bn, s_mv, s_std, s_rstd, s_nmr = (sem(n) for n in ("s_bn2", "s_mv2", "s_std2", "s_rstd2", "s_nmr2"))
        s_xn, s_xg, s_y = sem("s_xn2"), sem("s_xg2"), sem("s_y2")
        s_out = sem("s_out2")
        block = ctx.enter_context(nc.Block())

        @block.sync
        def _(sp):
            for t in range(NT):
                sp.dma_start(v[:, t], acc_scr[t * P:(t + 1) * P, :]).then_inc(s_in[t], 16)
            for t in range(NT):
                n = P if t < NT - 1 else TAIL
                sp.wait_ge(s_y, t + 1)
                sp.dma_start(y_out[t * P:t * P + n, :], v[0:n, t]).then_inc(s_out, 16)
            sp.wait_ge(s_out, 16 * NT)

        @block.gpsimd
        def _(pool):
            for t in range(NT):
                pool.wait_ge(s_xg, t + 1)
                pool.tensor_tensor(v[:, t], v[:, t], ln_sb[:, 3], ALU.add).then_inc(s_y, 1)

        @block.scalar
        def _(act):
            for t in range(NT):
                act.wait_ge(s_mv, t + 1)
                act.activation(std[:, t:t + 1], mv[:, t, 1:2], ACT.Sqrt, bias=eps[:]).then_inc(s_std, 1)
                act.wait_ge(s_nmr, t + 1)
                act.activation(v[:, t], v[:, t], ACT.Identity, scale=rstd[:, t:t + 1],
                               bias=nmr[:, t:t + 1]).then_inc(s_xn, 1)

        @block.vector
        def _(dve):
            dve.memset(eps[:], LN_EPS)
            for t in range(NT):
                dve.wait_ge(s_in[t], 16)
                for f in range(2):
                    ins = dve.bn_stats(stats[:, t, f], v[:, t, f * 512:f * 512 + 512])
                ins.then_inc(s_bn, 1)
                dve.wait_ge(s_bn, t + 1)
                dve.bn_aggr(mv[:, t], stats[:, t]).then_inc(s_mv, 1)
                if t:
                    dve.wait_ge(s_xn, t)
                    dve.tensor_tensor(v[:, t - 1], v[:, t - 1], ln_sb[:, 2], ALU.mult).then_inc(s_xg, 1)
                dve.wait_ge(s_std, t + 1)
                dve.reciprocal(rstd[:, t:t + 1], std[:, t:t + 1]).then_inc(s_rstd, 1)
                dve.wait_ge(s_rstd, t + 1)
                dve.scalar_tensor_tensor(out=nmr[:, t:t + 1], in0=mv[:, t, 0:1], scalar=-1.0,
                                         in1=rstd[:, t:t + 1], op0=ALU.mult, op1=ALU.mult).then_inc(s_nmr, 1)
            dve.wait_ge(s_xn, NT)
            dve.tensor_tensor(v[:, NT - 1], v[:, NT - 1], ln_sb[:, 2], ALU.mult).then_inc(s_xg, 1)


def program(nc, x_t, x_rows, w_in, w_lru, chan, w_out, w_router, ln, w13, w2, consts_in, y_out, states):
    y_scr = nc.dram_tensor("y_scr", (KT, P, ROWS), F32, kind="Internal").ap()
    x1_scr = nc.dram_tensor("x1_scr", (ROWS + P, D), F32, kind="Internal").ap()
    acc_scr = nc.dram_tensor("acc_scr", (ROWS + P, D), F32, kind="Internal").ap()
    mixer_phase(nc, x_t, w_in, w_lru, chan, y_scr, states)
    with (nc.sbuf_tensor("consts_sb", [P, NCONST], F32) as consts, nc.sbuf_tensor("ln_sb", [P, 4, D], F32) as ln_sb,
          nc.sbuf_tensor("logits", [P, NT, NR], F32) as logits, nc.sbuf_tensor("ids", [P, STEPS], I32) as ids,
          nc.sbuf_tensor("gates", [P, STEPS], F32) as gates, nc.sbuf_tensor("plan", [1, 3, STEPS], I32) as plan):
        project_phase(nc, y_scr, x_rows, w_out, w_router, ln, consts_in, x1_scr, acc_scr, consts, ln_sb, logits)
        route_phase(nc, consts, logits, ids, gates, plan)
        experts_phase(nc, x1_scr, acc_scr, w13, w2, consts, ids, gates, plan)
        finish_phase(nc, acc_scr, y_out, ln_sb)


def lay_out(inputs):
    import numpy as np
    a = {k: np.asarray(v) for k, v in inputs.items()}
    x = np.zeros((ROWS, D), np.float32)
    x[:SEQ], x[SEQ:TOK] = a["x_prompt"][0], a["x_sample"][0]
    out = {"x_rows": x}
    out["x_t"] = x[:TOK].reshape(TOK, KT, P).transpose(2, 1, 0)
    w = a["w_in"][0].reshape(KT, P, 5, GROUPS, P)[:, :, [3, 1, 2, 0, 4]]
    out["w_in"] = w.transpose(3, 2, 1, 0, 4).reshape(GROUPS * MT, P, KT, P)
    lru = np.zeros((GROUPS, P, 2, P), np.float32)
    half = P // 2
    for g, name in enumerate(("lru_wa", "lru_wx")):
        for head in range(2 * GROUPS):
            s = half * (head % 2)
            lru[head // 2, s:s + half, g, s:s + half] = a[name][0, head]
    out["w_lru"] = lru
    cols = [*a["conv_a_w"][0], *a["conv_b_w"][0], a["conv_b_bias"][0], a["lru_ba"][0], a["lru_bx"][0],
            a["lru_lambda"][0], *a["state_conv_a"][0, 0], *a["state_conv_b"][0, 0], a["state_lru_h"][0, 0]]
    out["chan"] = np.stack(cols, -1).reshape(GROUPS, P, NCOL).transpose(1, 0, 2)
    out["w_out"] = a["w_out"][0].reshape(KT, P, D).transpose(1, 0, 2)
    wr = np.concatenate([a["w_router_group"][0], a["w_router_expert"][0]], -1)
    out["w_router"] = wr.reshape(KT, P, NR).transpose(1, 0, 2)
    out["ln"] = np.broadcast_to(np.stack([a[n][0] for n in ("ln1_g", "ln1_b", "ln2_g", "ln2_b")]), (P, 4, D))
    w13 = np.concatenate([a["moe_w1"][0], a["moe_w3"][0]], -1)
    out["w13"] = w13.reshape(NE, KT, P, 2 * FE).transpose(0, 2, 1, 3)
    out["w2"] = a["moe_w2"][0].reshape(NE, FT, P, D).transpose(0, 2, 1, 3)
    out["consts"] = constants(np)
    return out


def constants(np):
    c = np.zeros((P, NCONST), np.float32)
    p = np.arange(P)
    c[:, C_ID:C_ID + P] = np.eye(P)
    c[:, C_TRI:C_TRI + P] = p[:, None] < p[None]
    c[:, C_ONE:C_ONE + P] = 1
    c[:, C_IO:C_IO + P] = p
    c[:, C_DEC:C_DEC + NG] = NG - np.arange(NG)
    c[:, C_THR:C_THR + NT] = P * np.arange(NT)
    token = np.arange(NT) * P + p[:, None]
    c[:, C_TOK:C_TOK + NT] = token + 1
    c[:, C_VAL:C_VAL + NT] = token < TOK
    c[:, C_INV:C_INV + NT] = (token >= TOK) * 2.0 ** 17
    c[:, C_SEG:C_SEG + NT * NE] = np.arange(NT * NE) % NT != 0
    c[:, C_PAD] = ROWS + p + 1
    return c


def states_of(s):
    rows = s.transpose(2, 1, 0).reshape(NST, GROUPS * P)
    return [rows[SA_P:SA_P + 2].reshape(1, 1, 2, -1), rows[SB_P:SB_P + 3].reshape(1, 1, 3, -1), rows[SH_P].reshape(1, 1, -1),
            rows[SA_S:SA_S + 2].reshape(1, 1, 2, -1), rows[SB_S:SB_S + 3].reshape(1, 1, 3, -1), rows[SH_S].reshape(1, 1, -1)]


_INS = ("x_t", "x_rows", "w_in", "w_lru", "chan", "w_out", "w_router", "ln", "w13", "w2", "consts")
_OUTS = (("y_out", (TOK, D)), ("states", (P, GROUPS, NST)))


def kernel(**inputs):
    import numpy as np
    from concourse import bacc
    from concourse.bass_utils import run_bass_kernel_spmd

    laid = lay_out(inputs)
    nc = bacc.Bacc("TRN2", target_bir_lowering=False, num_devices=1)
    arrays = {f"in_{n}": np.ascontiguousarray(laid[n]) for n in _INS}
    args = [nc.dram_tensor(f"in_{n}", arrays[f"in_{n}"].shape, F32, kind="ExternalInput").ap() for n in _INS]
    args += [nc.dram_tensor(f"out_{n}", shape, F32, kind="ExternalOutput").ap() for n, shape in _OUTS]
    program(nc, *args)
    got = run_bass_kernel_spmd(nc, [arrays], core_ids=[0]).results[0]
    y = got["out_y_out"]
    return (y[:SEQ].reshape(1, SEQ, D), y[SEQ:].reshape(1, DEC, D), *states_of(got["out_states"]))
```

```python
from contextlib import ExitStack

import concourse.bass as bass
from concourse import mybir

F32 = mybir.dt.float32
F32R = mybir.dt.float32r
I32 = mybir.dt.int32
ALU = mybir.AluOpType
ACT = mybir.ActivationFunctionType
AX = mybir.AxisListType

P = 128
D = 1024
KT = D // P
SEQ, DEC = 2048, 32
TOK = SEQ + DEC
CHUNK = 416
NCH = TOK // CHUNK
HEAD = SEQ - (NCH - 1) * CHUNK
GAP = 3
EXT = HEAD + GAP + DEC
LRU_N = EXT + 1
GROUPS = 4
MT = 5
WP = MT + 1
XP = KT // 2
NT = -(-TOK // P)
TAIL = TOK - (NT - 1) * P
ROWS = NT * P
NG, NE_G, NE = 4, 4, 16
FE = 256
FT = FE // P
TOPK = 2
STEPS = (TOPK * TOK + NE * P) // P
NR = NG + NE
ALPHA = 2.0 ** 0.25
LN_EPS = 1e-5
GELU_A, GELU_B = 0.7978845608028654, 0.7978845608028654 * 0.044715
PARTS = ((0, slice(0, 5)), (0, slice(5, NT)), (1, slice(0, NT)))
(CA0, CA1, CA2, CB0, CB1, CB2, CB3, CBIAS, RBIAS, IBIAS, LAM, HA0, HA1, HB0, HB1, HB2, HPREV, NCOL) = range(18)
SA_P, SB_P, SA_S, SB_S, SH_P, SH_S, NST = 0, 2, 5, 7, 10, 11, 12
C_ID, C_TRI, C_ONE, C_IO = 0, P, 2 * P, 3 * P
C_DEC = 4 * P
C_THR, C_TOK, C_VAL, C_INV = (C_DEC + NG + NT * i for i in range(4))
C_SEG = C_INV + NT
NSMALL = C_SEG - C_DEC
C_PAD = C_SEG + NT * NE
NCONST = C_PAD + 1


class Mixer:
    pass


def mixer(nc, ctx, x_t, w_in, w_lru, w_out, chan, y_scr, states, x_rows):
    def sb(name, shape, dt=F32):
        return ctx.enter_context(nc.sbuf_tensor(name, shape, dt))

    def sem(name):
        return ctx.enter_context(nc.semaphore(name))

    shapes = ("x_hi", [P, KT, TOK]), ("x_lo", [P, KT, TOK]), ("w_hi", [P, MT, KT, P]), ("w_lo", [P, MT, KT, P])
    with ExitStack() as own:
        x_hi, x_lo, w_hi, w_lo = (own.enter_context(nc.sbuf_tensor(n, shape, F32R)) for n, shape in shapes)
    x_hi_p, x_lo_p, w_hi_p, w_lo_p = (sb(n + "_p", shape) for n, shape in shapes)
    l_hi = sb("l_hi", [P, 2, P], F32R)
    l_lo = sb("l_lo", [P, 2, P], F32R)
    w_raw = sb("w_raw", [P, 2, KT, P])
    x_raw = sb("x_raw", [P, 2, 2, CHUNK])
    par = sb("par", [P, GROUPS, NCOL])
    vb = sb("vb", [P, 3 + EXT + 2])
    u = sb("u", [P, 2 + EXT + 1])
    xc = sb("xc", [P, LRU_N])
    xc_hi = sb("xc_hi", [P, LRU_N], F32R)
    xc_lo = sb("xc_lo", [P, LRU_N], F32R)
    ya = sb("ya", [P, EXT + 1])
    gel = sb("gel", [P, CHUNK])
    yb = sb("yb", [P, LRU_N])
    a_t = sb("a_t", [P, LRU_N])
    b_t = sb("b_t", [P, LRU_N])
    i_t = sb("i_t", [P, LRU_N])
    h_carry = sb("h_carry", [P, 1])
    stash = sb("stash", [P, GROUPS, NST])
    sp4 = sb("sp4", [P, GROUPS])
    nsp4 = sb("nsp4", [P, GROUPS])
    hrb = sb("hrb", [P, GROUPS])
    hib = sb("hib", [P, GROUPS])
    sp_t = sb("sp_t", [P, 8, GROUPS])

    ps_vb_c = ctx.enter_context(nc.psum_tensor("ps_vb_c", [P, 2, 512], F32))
    ps_va_b = ctx.enter_context(nc.psum_tensor("ps_va_b", [P, 2, 512], F32))
    ps_r_i = ctx.enter_context(nc.psum_tensor("ps_r_i", [P, 2, 512], F32))
    ps_g = ctx.enter_context(nc.psum_tensor("ps_g", [P, 512], F32))
    ps_vb, ps_c, ps_va, ps_b, ps_r, ps_i = (t[:, i] for t in (ps_vb_c, ps_va_b, ps_r_i) for i in range(2))
    ps = [ps_vb, ps_c, ps_va, ps_b, ps_g]
    wo_hi, wo_lo = x_hi[:, :, 0:D], x_lo[:, :, 0:D]
    tile_at = lambda t, base: [t[:, :, base + i * P:base + (i + 1) * P] for i in range(2)]
    y_hi, y_lo = tile_at(x_hi, D), tile_at(x_lo, D)
    y_raw = tile_at(x_hi_p, D + 2 * P)
    x1_t = tile_at(x_lo_p, D + 2 * P)
    ident, wr = x_lo_p[:, 0, D + 4 * P:D + 5 * P], x_hi_p[:, :, D + 4 * P:D + 4 * P + NR]
    row = lambda t, i: t[:, i].rearrange("p k n -> p (k n)")
    x_in, s_sb = [row(w_hi_p, i) for i in (0, 1)], [row(w_hi_p, i) for i in (2, 3)]
    x1, ax1 = [row(w_lo_p, i) for i in (0, 1)], [row(w_lo_p, i) for i in (2, 3)]
    ln_g, ln_b = row(w_hi_p, 4), row(w_lo_p, 4)
    assert D + 5 * P <= (NCH - 1) * CHUNK and XP * 2 == KT and MT == 5 and P * KT == D

    s_w0 = sem("s_w0")
    s_yraw = [sem(f"s_yraw{i}") for i in range(2)]
    s_yhi, s_ylo = sem("s_yhi"), sem("s_ylo")
    s_x = [sem(f"s_xin{i}") for i in range(2)]
    s_par = sem("s_par")
    s_wraw = [sem(f"s_wraw{i}") for i in range(2)]
    s_xraw = [sem(f"s_xraw{i}") for i in range(2)]
    s_whi, s_wlo = sem("s_whi"), sem("s_wlo")
    s_xhi, s_xlo = sem("s_xhi"), sem("s_xlo")
    s_mm = [sem(f"s_mm{i}") for i in range(MT)]
    s_ri = sem("s_ri")
    s_vb = sem("s_vb")
    s_hist = sem("s_hist")
    s_tapb = sem("s_tapb")
    s_convb = sem("s_convb")
    s_xch, s_xcl = sem("s_xch"), sem("s_xcl")
    s_c = sem("s_c")
    s_u = sem("s_u")
    s_tapa = sem("s_tapa")
    s_conva = sem("s_conva")
    s_ya = sem("s_ya")
    s_ya_out, s_yb_out = sem("s_ya_out"), sem("s_yb_out")
    s_gsq, s_gp, s_gt, s_gel = sem("s_gsq"), sem("s_gp"), sem("s_gt"), sem("s_gel")
    s_thr, s_thi = sem("s_thr"), sem("s_thi")
    s_a, s_t = sem("s_a"), sem("s_t")
    s_z, s_sq = sem("s_z"), sem("s_sq")
    s_m = sem("s_m")
    s_b = sem("s_b")
    s_fix = sem("s_fix")
    s_h = sem("s_h")
    s_yb = sem("s_yb")
    s_sp = sem("s_sp")
    s_spe = sem("s_spe")
    s_tail = sem("s_tail")
    s_carry = sem("s_carry")
    s_st = sem("s_st")
    s_st_out = sem("s_st_out")

    def segs(last):
        return [(0, 0, HEAD), (HEAD, HEAD + GAP, DEC)] if last else [(0, 0, CHUNK)]

    W_OUT = GROUPS * WP
    READ = (GROUPS - 1) * NCH + NCH - 2

    def mix_gpsimd(pool):
        pool.dma_start(par[:], chan).then_inc(s_par, 16)
        for i in range(1, WP):
            if i >= 2:
                pool.wait_ge(s_wlo, i - 1)
            dst = w_raw[:, i % 2] if i < MT else w_raw[:, i % 2, 0:2]
            src = w_in[i] if i < MT else w_lru[0]
            pool.dma_start(dst, src).then_inc(s_wraw[i % 2], 16)
        with pool.Fori(1, GROUPS) as j:
            for i in range(WP):
                pool.wait_ge(s_wlo, j * WP + (i - 1))
                if i < MT:
                    pool.dma_start(w_raw[:, i % 2],
                                   w_in[bass.ds(j * MT + i, 1)].rearrange("o p k n -> p (o k) n")).then_inc(s_wraw[i % 2], 16)
                else:
                    pool.dma_start(w_raw[:, i % 2, 0:2],
                                   w_lru[bass.ds(j, 1)].rearrange("o p k n -> p (o k) n")).then_inc(s_wraw[i % 2], 16)
        for k in range(KT):
            pool.wait_ge(s_wlo, W_OUT + (k - 1))
            pool.dma_start(w_raw[:, k % 2].rearrange("p k n -> p (k n)"), w_out[:, k]).then_inc(s_wraw[k % 2], 16)

    def mix_sync(sp):
        def load_x(c, pieces):
            for n in pieces:
                if not (isinstance(c, int) and c == 0 and n < 2):
                    sp.wait_ge(s_xlo, c * XP + (n - 1))
                sp.dma_start(x_raw[:, n % 2], x_t[:, 2 * n:2 * n + 2, bass.ds(c * CHUNK, CHUNK)]).then_inc(s_xraw[n % 2], 16)

        def store_y(j, c, last):
            q = j * NCH + c
            for src, s_ready, s_out, half in ((ya, s_ya, s_ya_out, 0), (yb, s_yb, s_yb_out, GROUPS)):
                sp.wait_ge(s_ready, q + 1)
                row = y_scr[bass.ds(j + half, 1)].rearrange("o p t -> p (o t)")
                if last:
                    sp.dma_start(row[:, SEQ - HEAD:SEQ], src[:, 0:HEAD]).then_inc(s_out, 16)
                    sp.dma_start(row[:, SEQ:TOK], src[:, HEAD + GAP:EXT]).then_inc(s_out, 16)
                else:
                    sp.dma_start(row[:, bass.ds(c * CHUNK, CHUNK)], src[:, 0:CHUNK]).then_inc(s_out, 16)

        sp.dma_start(w_raw[:, 0], w_in[0]).then_inc(s_w0, 16)
        early, late = range(XP // 2), range(XP // 2, XP)
        for c in range(2):
            load_x(c, range(XP))
        load_x(2, early)
        with sp.Fori(0, NCH - 3) as c:
            store_y(0, c, False)
            load_x(c + 2, late)
            load_x(c + 3, early)
        store_y(0, NCH - 3, False)
        load_x(NCH - 1, late)
        store_y(0, NCH - 2, False)
        store_y(0, NCH - 1, True)
        with sp.Fori(1, GROUPS - 1) as j:
            with sp.Fori(0, NCH - 1) as c:
                store_y(j, c, False)
            store_y(j, NCH - 1, True)
        with sp.Fori(0, NCH - 1) as c:
            store_y(GROUPS - 1, c, False)
        stored = 16 * (GROUPS * (NCH + 1) - 2)
        sp.wait_ge(s_ya_out, stored)
        sp.wait_ge(s_yb_out, stored)
        sp.wait_ge(s_mm[MT - 1], READ + 1)
        for t in range(2):
            sp.dma_start(y_raw[t], y_scr[:, :, t * P:t * P + P].rearrange("k p t -> p k t")).then_inc(s_yraw[t], 16)
        for t in range(2):
            sp.wait_ge(s_mm[t], GROUPS * NCH)
            sp.dma_start(x_in[t], x_rows[t * P:t * P + P, :]).then_inc(s_x[t], 16)
        store_y(GROUPS - 1, NCH - 1, True)
        sp.wait_ge(s_st, GROUPS)
        sp.dma_start(states, stash[:]).then_inc(s_st_out, 16)
        sp.wait_ge(s_ya_out, 16 * GROUPS * (NCH + 1))
        sp.wait_ge(s_yb_out, 16 * GROUPS * (NCH + 1))

    def mix_tensor(pe):
        def step(j, c):
            q = j * NCH + c
            start = isinstance(q, int) and q == 0
            fresh = isinstance(q, int) and q < 2
            if not fresh:
                pe.wait_ge(s_xlo, (c + 1) * XP)
            free = (s_vb, s_c, s_u, s_ya, s_gel)
            for i in range(MT):
                pe.wait_ge(s_wlo, j * WP + (i + 1))
                if not start:
                    pe.wait_ge(free[i], q)
                for k in range(KT):
                    if fresh and i == 0 and k % 2 == 0:
                        pe.wait_ge(s_xlo, c * XP + (k // 2 + 1))
                    for n, (w, x) in enumerate(((w_hi, x_hi), (w_hi, x_lo), (w_lo, x_hi))):
                        mm = pe.matmul(ps[i][:, 0:CHUNK], w[:, i, k], x[:, k, bass.ds(c * CHUNK, CHUNK)],
                                       start=(k == 0 and n == 0), stop=(k == KT - 1 and n == 2))
                mm.then_inc(s_mm[i], 1)
            pe.wait_ge(s_wlo, j * WP + WP)
            pe.wait_ge(s_xcl, q + 1)
            if not start:
                pe.wait_ge(s_thi, q)
            for g, bank in enumerate((ps_r, ps_i)):
                for n, (w, x) in enumerate(((l_hi, xc_hi), (l_hi, xc_lo), (l_lo, xc_hi))):
                    mm = pe.matmul(bank[:, 0:LRU_N], w[:, g], x[:], start=(n == 0), stop=(n == 2))
            mm.then_inc(s_ri, 1)

        step(0, 0)
        step(0, 1)
        with pe.Fori(2, NCH) as c:
            step(0, c)
        with pe.Fori(1, GROUPS) as j:
            with pe.Fori(0, NCH) as c:
                step(j, c)

    def raw_piece(i):
        return (w_raw[:, i % 2], w_hi[:, i], w_lo[:, i]) if i < MT else (w_raw[:, i % 2, 0:2], l_hi[:], l_lo[:])

    def mix_scalar(act):
        def split_w(j, i):
            raw, hi, _ = raw_piece(i)
            if isinstance(j, int) and j == 0 and i == 0:
                act.wait_ge(s_w0, 16)
            else:
                act.wait_ge(s_wraw[i % 2], 16 * (j * (WP // 2) + (i // 2 + i % 2)))
            act.wait_ge(s_mm[i] if i < MT else s_ri, j * NCH)
            act.activation(hi, raw, ACT.Copy).then_inc(s_whi, 1)

        def split_w_out(k):
            if k < KT:
                act.wait_ge(s_wraw[k % 2], 16 * (W_OUT // 2 + (k // 2 + k % 2)))
                act.wait_ge(s_mm[MT - 1], READ)
                act.activation(wo_hi[:, k], w_raw[:, k % 2].rearrange("p k n -> p (k n)"), ACT.Copy).then_inc(s_whi, 1)
            elif k < KT + 2:
                act.wait_ge(s_yraw[k - KT], 16)
                act.activation(y_hi[k - KT], y_raw[k - KT], ACT.Copy).then_inc(s_yhi, 1)

        def split_x(c, n):
            act.wait_ge(s_xraw[n % 2], 16 * (c * (XP // 2) + (n // 2 + 1)))
            act.activation(x_hi[:, 2 * n:2 * n + 2, bass.ds(c * CHUNK, CHUNK)], x_raw[:, n % 2], ACT.Copy).then_inc(s_xhi, 1)

        def step(j, c, last, split):
            q = j * NCH + c
            col = lambda n: par[:, bass.ds(j, 1), n]
            act.wait_ge(s_mm[0], q + 1)
            act.wait_ge(s_hist, q + 1)
            for k, (s, d, n) in enumerate(segs(last)):
                ins = act.activation(vb[:, 3 + d:3 + d + n], ps_vb[:, s:s + n], ACT.Copy)
            ins.then_inc(s_vb, 1)
            if split is not None:
                split(0)
            n = EXT if last else CHUNK
            act.wait_ge(s_vb, q + 1)
            act.wait_ge(s_m, q)
            act.activation(xc[:, 0:n], vb[:, 0:n], ACT.Identity, scale=col(CB0), bias=col(CBIAS)).then_inc(s_tapb, 1)
            act.wait_ge(s_mm[1], q + 1)
            act.wait_ge(s_ya_out, 16 * (q + j))
            act.activation(ya[:, 0:CHUNK], ps_c[:, 0:CHUNK], ACT.Copy).then_inc(s_c, 1)
            if split is not None:
                split(1)
            act.wait_ge(s_convb, 3 * q + 3)
            act.wait_ge(s_ri, q)
            act.activation(xc_hi[:], xc[:], ACT.Copy).then_inc(s_xch, 1)
            act.wait_ge(s_u, q + 1)
            act.activation(ya[:, 0:n], u[:, 0:n], ACT.Copy, scale=col(CA0)).then_inc(s_tapa, 1)
            if split is not None:
                split(2)
                split(3)
            act.wait_ge(s_mm[4], q + 1)
            act.wait_ge(s_yb, q)
            act.activation(gel[:], ps_g[:, 0:CHUNK], ACT.Square).then_inc(s_gsq, 1)
            act.wait_ge(s_gp, 2 * q + 2)
            act.activation(gel[:], gel[:], ACT.Tanh).then_inc(s_gt, 1)
            if split is not None:
                split(4)
            act.wait_ge(s_ri, q + 1)
            act.wait_ge(s_yb_out, 16 * (q + j))
            act.activation(yb[:], ps_r[:, 0:LRU_N], ACT.Tanh, scale=0.5, bias=hrb[:, bass.ds(j, 1)]).then_inc(s_thr, 1)
            act.wait_ge(s_b, q)
            act.activation(i_t[:], ps_i[:, 0:LRU_N], ACT.Tanh, scale=0.5, bias=hib[:, bass.ds(j, 1)]).then_inc(s_thi, 1)
            act.wait_ge(s_thr, q + 1)
            act.wait_ge(s_h, q)
            act.activation(a_t[:], yb[:], ACT.Exp, scale=nsp4[:, bass.ds(j, 1)], bias=nsp4[:, bass.ds(j, 1)]).then_inc(s_a, 1)
            act.wait_ge(s_a, q + 1)
            act.activation(yb[:], yb[:], ACT.Tanh, scale=sp4[:, bass.ds(j, 1)], bias=sp4[:, bass.ds(j, 1)]).then_inc(s_t, 1)
            if split is not None:
                split(5)
            act.wait_ge(s_z, 2 * q + 2)
            act.activation(yb[:], yb[:], ACT.Sqrt).then_inc(s_sq, 1)

        split_w(0, 0)
        for n in range(XP):
            split_x(0, n)
        split_w(0, 1)
        split_w(0, 2)

        def first(i):
            if i < 3:
                split_w(0, 3 + i)
            if i in (2, 3):
                for n in range(XP // 2):
                    split_x(1, (i - 2) * (XP // 2) + n)
            if i == 3:
                act.wait_ge(s_sp, 1)
                act.activation(sp_t[:, 1], sp_t[:, 0], ACT.Exp, scale=-1.0).then_inc(s_spe, 1)
            if i == 4:
                act.wait_ge(s_sp, 15)

        step(0, 0, False, first)
        with act.Fori(1, NCH - 1) as c:
            step(0, c, False, lambda i: split_x(c + 1, i) if i < XP else None)
        step(0, NCH - 1, True, lambda i: split_w(1, i))
        with act.Fori(1, GROUPS - 1) as j:
            with act.Fori(0, NCH - 1) as c:
                step(j, c, False, None)
            step(j, NCH - 1, True, lambda i: split_w(j + 1, i))
        def last_splits(i):
            for k in ((4, 5), (6,), (7,), (8, 9), (), ())[i]:
                split_w_out(k)

        with act.Fori(0, NCH - 2) as c:
            step(GROUPS - 1, c, False, None)
        step(GROUPS - 1, NCH - 2, False, lambda i: split_w_out(i) if i < XP else None)
        step(GROUPS - 1, NCH - 1, True, last_splits)

    def mix_vector(dve):
        def split_w(j, i):
            raw, hi, lo = raw_piece(i)
            dve.wait_ge(s_whi, j * WP + (i + 1))
            dve.tensor_tensor(lo, raw, hi.bitcast(F32), ALU.subtract).then_inc(s_wlo, 1)

        def split_w_out(k):
            if k < KT:
                dve.wait_ge(s_whi, W_OUT + (k + 1))
                dve.tensor_tensor(wo_lo[:, k], w_raw[:, k % 2].rearrange("p k n -> p (k n)"),
                                  wo_hi[:, k].bitcast(F32), ALU.subtract).then_inc(s_wlo, 1)
            elif k < KT + 2:
                dve.wait_ge(s_yhi, k - KT + 1)
                dve.tensor_tensor(y_lo[k - KT], y_raw[k - KT], y_hi[k - KT].bitcast(F32), ALU.subtract).then_inc(s_ylo, 1)

        def split_x(c, n):
            dve.wait_ge(s_xhi, c * XP + (n + 1))
            at = bass.ds(c * CHUNK, CHUNK)
            dve.tensor_tensor(x_lo[:, 2 * n:2 * n + 2, at], x_raw[:, n % 2],
                              x_hi[:, 2 * n:2 * n + 2, at].bitcast(F32), ALU.subtract).then_inc(s_xlo, 1)

        def step(j, c, last, split):
            q = j * NCH + c
            n = EXT if last else CHUNK
            col = lambda m: par[:, bass.ds(j, 1), m]
            if split is not None:
                split(0)
            for k in range(1, 4):
                if k == 1:
                    dve.wait_ge(s_tapb, q + 1)
                else:
                    dve.wait_ge(s_convb, 3 * q + (k - 1))
                dve.scalar_tensor_tensor(out=xc[:, 0:n], in0=vb[:, k:k + n], scalar=col(CB0 + k), in1=xc[:, 0:n],
                                         op0=ALU.mult, op1=ALU.add).then_inc(s_convb, 1)
            if split is not None:
                split(1)
            dve.wait_ge(s_xch, q + 1)
            dve.tensor_tensor(xc_lo[:], xc[:], xc_hi[:].bitcast(F32), ALU.subtract).then_inc(s_xcl, 1)
            dve.wait_ge(s_c, q + 1)
            dve.wait_ge(s_mm[2], q + 1)
            dve.wait_ge(s_hist, q + 1)
            for s, d, m in segs(last):
                ins = dve.tensor_tensor(u[:, 2 + d:2 + d + m], ps_va[:, s:s + m], ya[:, s:s + m], ALU.mult)
            ins.then_inc(s_u, 1)
            for k in range(1, 3):
                if k == 1:
                    dve.wait_ge(s_tapa, q + 1)
                else:
                    dve.wait_ge(s_conva, 2 * q + 1)
                dve.scalar_tensor_tensor(out=ya[:, 0:n], in0=u[:, k:k + n], scalar=col(CA0 + k), in1=ya[:, 0:n],
                                         op0=ALU.mult, op1=ALU.add).then_inc(s_conva, 1)
            if split is not None:
                split(2)
                split(3)
            dve.wait_ge(s_mm[3], q + 1)
            dve.wait_ge(s_conva, 2 * q + 2)
            for s, d, m in segs(last):
                ins = dve.tensor_tensor(ya[:, d:d + m], ya[:, d:d + m], ps_b[:, s:s + m], ALU.mult)
            ins.then_inc(s_ya, 1)
            if last:
                st = lambda a, m: stash[:, bass.ds(j, 1), a:a + m].rearrange("p o m -> p (o m)")
                dve.tensor_copy(st(SA_P, 2), u[:, HEAD:HEAD + 2])
                dve.tensor_copy(st(SA_S, 2), u[:, EXT:EXT + 2])
                dve.tensor_copy(st(SB_P, 3), vb[:, HEAD:HEAD + 3])
                dve.tensor_copy(st(SB_S, 3), vb[:, EXT:EXT + 3]).then_inc(s_tail, 1)
                dve.wait_ge(s_tail, q + 1)
                dve.memset(u[:, 0:2], 0.0)
                dve.memset(vb[:, 0:3], 0.0).then_inc(s_hist, 1)
            else:
                dve.tensor_copy(u[:, 0:2], u[:, CHUNK:CHUNK + 2])
                dve.tensor_copy(vb[:, 0:3], vb[:, CHUNK:CHUNK + 3]).then_inc(s_tail, 1)
                dve.wait_ge(s_tail, q + 1)
                grp = lambda a, m: par[:, bass.ds(j, 1), a:a + m].rearrange("p o m -> p (o m)")
                dve.tensor_copy(u[:, HEAD + 2:HEAD + 3], grp(HA0, 1))
                dve.tensor_copy(u[:, HEAD + 3:HEAD + 5], grp(HA0, 2))
                dve.tensor_copy(vb[:, HEAD + 3:HEAD + 6], grp(HB0, 3)).then_inc(s_hist, 1)
            dve.wait_ge(s_gsq, q + 1)
            dve.tensor_scalar(gel[:], gel[:], GELU_B, GELU_A, ALU.mult, ALU.add).then_inc(s_gp, 1)
            dve.wait_ge(s_gp, 2 * q + 1)
            dve.tensor_tensor(gel[:], gel[:], ps_g[:, 0:CHUNK], ALU.mult).then_inc(s_gp, 1)
            if split is not None:
                split(4)
            dve.wait_ge(s_gt, q + 1)
            dve.scalar_tensor_tensor(out=gel[:], in0=gel[:], scalar=1.0, in1=ps_g[:, 0:CHUNK],
                                     op0=ALU.add, op1=ALU.mult).then_inc(s_gel, 1)
            dve.wait_ge(s_a, q + 1)
            dve.tensor_tensor(b_t[:], a_t[:], a_t[:], ALU.mult).then_inc(s_z, 1)
            dve.wait_ge(s_z, 2 * q + 1)
            dve.wait_ge(s_t, q + 1)
            dve.scalar_tensor_tensor(out=yb[:], in0=b_t[:], scalar=1.0, in1=yb[:],
                                     op0=ALU.add, op1=ALU.mult).then_inc(s_z, 1)
            dve.wait_ge(s_thi, q + 1)
            dve.scalar_tensor_tensor(out=i_t[:], in0=i_t[:], scalar=1.0, in1=xc[:],
                                     op0=ALU.add, op1=ALU.mult).then_inc(s_m, 1)
            if split is not None:
                split(5)
            dve.wait_ge(s_sq, q + 1)
            dve.wait_ge(s_m, q + 1)
            dve.scalar_tensor_tensor(out=b_t[:], in0=yb[:], scalar=0.5, in1=i_t[:],
                                     op0=ALU.mult, op1=ALU.mult).then_inc(s_b, 1)
            dve.wait_ge(s_b, q + 1)
            if last:
                dve.memset(a_t[:, HEAD:HEAD + GAP], 0.0)
                dve.memset(b_t[:, HEAD:HEAD + GAP - 1], 0.0)
                dve.tensor_copy(b_t[:, HEAD + GAP - 1:HEAD + GAP], col(HPREV)).then_inc(s_fix, 1)
                dve.wait_ge(s_fix, j + 1)
            dve.wait_ge(s_carry, q + 1)
            dve.tensor_tensor_scan(yb[:, 0:n], a_t[:, 0:n], b_t[:, 0:n], h_carry[:], ALU.mult, ALU.add).then_inc(s_h, 1)
            dve.wait_ge(s_h, q + 1)
            if last:
                dve.tensor_copy(st(SH_P, 1), yb[:, HEAD - 1:HEAD])
                dve.tensor_copy(st(SH_S, 1), yb[:, EXT - 1:EXT]).then_inc(s_st, 1)
                dve.memset(h_carry[:], 0.0).then_inc(s_carry, 1)
            else:
                dve.tensor_copy(h_carry[:], yb[:, CHUNK - 1:CHUNK]).then_inc(s_carry, 1)
            dve.wait_ge(s_carry, q + 2)
            dve.wait_ge(s_gel, q + 1)
            for s, d, m in segs(last):
                ins = dve.scalar_tensor_tensor(out=yb[:, d:d + m], in0=yb[:, d:d + m], scalar=0.5, in1=gel[:, s:s + m],
                                               op0=ALU.mult, op1=ALU.mult)
            ins.then_inc(s_yb, 1)

        dve.memset(xc[:], 0.0)
        dve.memset(vb[:], 0.0)
        dve.memset(h_carry[:], 0.0).then_inc(s_carry, 1)
        dve.memset(u[:], 0.0).then_inc(s_hist, 1)
        split_w(0, 0)
        for n in range(XP):
            split_x(0, n)
        split_w(0, 1)
        split_w(0, 2)

        def softplus():
            dve.wait_ge(s_par, 16)
            lam = par[:, :, LAM]
            dve.scalar_tensor_tensor(out=sp_t[:, 0], in0=lam, scalar=-1.0, in1=lam, op0=ALU.mult, op1=ALU.max).then_inc(s_sp, 1)
            dve.wait_ge(s_spe, 1)
            dve.tensor_scalar(sp_t[:, 2], sp_t[:, 1], 2.0, None, ALU.add).then_inc(s_sp, 1)
            dve.wait_ge(s_sp, 2)
            dve.reciprocal(sp_t[:, 3], sp_t[:, 2]).then_inc(s_sp, 1)
            dve.wait_ge(s_sp, 3)
            dve.tensor_tensor(sp_t[:, 4], sp_t[:, 1], sp_t[:, 3], ALU.mult).then_inc(s_sp, 1)
            dve.wait_ge(s_sp, 4)
            dve.tensor_tensor(sp_t[:, 5], sp_t[:, 4], sp_t[:, 4], ALU.mult).then_inc(s_sp, 1)
            dve.wait_ge(s_sp, 5)
            dve.tensor_scalar(sp_t[:, 6], sp_t[:, 5], 1.0 / 15, None, ALU.mult).then_inc(s_sp, 1)
            for n, odd in enumerate((13, 11, 9, 7, 5, 3)):
                dve.wait_ge(s_sp, 6 + n)
                dve.scalar_tensor_tensor(out=sp_t[:, 6], in0=sp_t[:, 6], scalar=1.0 / odd, in1=sp_t[:, 5],
                                         op0=ALU.add, op1=ALU.mult).then_inc(s_sp, 1)
            dve.wait_ge(s_sp, 12)
            dve.scalar_tensor_tensor(out=sp_t[:, 6], in0=sp_t[:, 6], scalar=1.0, in1=sp_t[:, 4],
                                     op0=ALU.add, op1=ALU.mult)
            dve.tensor_scalar(sp_t[:, 7], lam, -1.0, 0.0, ALU.mult, ALU.max).then_inc(s_sp, 1)
            dve.wait_ge(s_sp, 13)
            dve.scalar_tensor_tensor(out=sp_t[:, 7], in0=sp_t[:, 6], scalar=2.0, in1=sp_t[:, 7],
                                     op0=ALU.mult, op1=ALU.add).then_inc(s_sp, 1)
            dve.wait_ge(s_sp, 14)
            dve.tensor_scalar(sp4[:], sp_t[:, 7], 4.0, None, ALU.mult)
            dve.tensor_scalar(nsp4[:], sp_t[:, 7], -4.0, None, ALU.mult)
            dve.tensor_scalar(hrb[:], par[:, :, RBIAS], 0.5, None, ALU.mult)
            dve.tensor_scalar(hib[:], par[:, :, IBIAS], 0.5, None, ALU.mult).then_inc(s_sp, 1)

        def first(i):
            if i < 3:
                split_w(0, 3 + i)
            if i in (2, 3):
                for n in range(XP // 2):
                    split_x(1, (i - 2) * (XP // 2) + n)
            if i == 3:
                softplus()

        step(0, 0, False, first)
        with dve.Fori(1, NCH - 1) as c:
            step(0, c, False, lambda i: split_x(c + 1, i) if i < XP else None)
        step(0, NCH - 1, True, lambda i: split_w(1, i))
        with dve.Fori(1, GROUPS - 1) as j:
            with dve.Fori(0, NCH - 1) as c:
                step(j, c, False, None)
            step(j, NCH - 1, True, lambda i: split_w(j + 1, i))
        def last_splits(i):
            for k in ((4, 5), (6,), (7,), (8, 9), (), ())[i]:
                split_w_out(k)

        with dve.Fori(0, NCH - 2) as c:
            step(GROUPS - 1, c, False, None)
        step(GROUPS - 1, NCH - 2, False, lambda i: split_w_out(i) if i < XP else None)
        step(GROUPS - 1, NCH - 1, True, last_splits)

    mx = Mixer()
    mx.engines = (mix_sync, mix_gpsimd, mix_tensor, mix_scalar, mix_vector)
    mx.banks = (ps_vb_c, ps_va_b, ps_r_i)
    mx.wo_hi, mx.wo_lo, mx.y_hi, mx.y_lo, mx.y_raw, mx.x1_t = wo_hi, wo_lo, y_hi, y_lo, y_raw, x1_t
    mx.x_in, mx.s_sb, mx.x1, mx.ax1 = x_in, s_sb, x1, ax1
    mx.ident, mx.wr, mx.ln_g, mx.ln_b = ident, wr, ln_g, ln_b
    mx.free = w_raw[:, 0].rearrange("p k n -> p (k n)")
    mx.s_yraw, mx.s_yhi, mx.s_ylo, mx.s_x = s_yraw, s_yhi, s_ylo, s_x
    mx.s_mm, mx.s_vb, mx.s_c, mx.s_u, mx.s_ya, mx.s_thi = s_mm, s_vb, s_c, s_u, s_ya, s_thi
    mx.s_wlo, mx.s_st_out = s_wlo, s_st_out
    return mx


def tiles(eng, emit):
    emit(0, 0, 0)
    emit(1, 1, 0)
    with eng.Fori(1, NT // 2) as h:
        emit(h * 2, 0, h)
        emit(h * 2 + 1, 1, h)
    emit(NT - 1, 0, NT // 2)


def mix_project_phase(nc, x_t, w_in, w_lru, chan, y_scr, states, x_rows, w_out, w_router, ln, consts_in,
                      x1_scr, acc_scr, logits, small):
    with ExitStack() as ctx:
        mx = mixer(nc, ctx, x_t, w_in, w_lru, w_out, chan, y_scr, states, x_rows)
        mix_sync, mix_gpsimd, mix_tensor, mix_scalar, mix_vector = mx.engines
        STEPS_MIX = GROUPS * NCH

        def sb(name, shape, dt=F32):
            return ctx.enter_context(nc.sbuf_tensor(name, shape, dt))

        def sem(name):
            return ctx.enter_context(nc.semaphore(name))

        ident, wr = mx.ident, mx.wr
        wo_hi, wo_lo, y_hi, y_lo, y_raw, x1_t = mx.wo_hi, mx.wo_lo, mx.y_hi, mx.y_lo, mx.y_raw, mx.x1_t
        x_in, s_sb, x1, ax1 = mx.x_in, mx.s_sb, mx.x1, mx.ax1
        ln_g, ln_b, zero = mx.ln_g, mx.ln_b, mx.free
        stats = sb("stats", [P, 2, 2, 6])
        mv = sb("mv", [P, 2, 2])
        std = sb("std", [P, 2])
        rstd = sb("rstd", [P, 2])
        nmr = sb("nmr", [P, 2])
        eps = sb("eps", [P, 1])
        ps_m = [mx.banks[i][:].rearrange("p b n -> p (b n)") for i in range(2)]
        ps_t = mx.banks[2][:].rearrange("p b (k n) -> p (b k) n", n=P)
        ps_l = ctx.enter_context(nc.psum_tensor("ps_l", [P, 512], F32))

        s_c = sem("s_const")
        s_sm = sem("s_small")
        s_ln = sem("s_ln1")
        s_yraw, s_yhi, s_ylo, s_x = mx.s_yraw, mx.s_yhi, mx.s_ylo, mx.s_x
        s_pad = sem("s_ypad")
        s_m = sem("s_pm")
        s_s = sem("s_s")
        s_bn, s_mv = sem("s_bn"), sem("s_mv")
        s_std, s_rstd, s_nmr = sem("s_std"), sem("s_rstd"), sem("s_nmr")
        s_xn, s_xg = sem("s_xn"), sem("s_xg")
        s_x1, s_ax = sem("s_x1"), sem("s_ax")
        s_x1o = [sem(f"s_x1o{i}") for i in range(2)]
        s_axo = [sem(f"s_axo{i}") for i in range(2)]
        s_tr, s_x1t = sem("s_tr"), sem("s_x1t")
        s_l, s_lo = sem("s_l"), sem("s_lev")
        s_z, s_zo = sem("s_zero"), sem("s_zo")
        block = ctx.enter_context(nc.Block())

        @block.gpsimd
        def _(pool):
            mix_gpsimd(pool)
            pool.wait_ge(mx.s_mm[MT - 1], STEPS_MIX - 1)
            pool.dma_start(ident, consts_in[:, C_ID:C_ID + P]).then_inc(s_c, 16)
            pool.dma_start(wr, w_router).then_inc(s_c, 16)
            pool.dma_start(small[:], consts_in[:, C_DEC:C_SEG]).then_inc(s_sm, 16)
            pool.wait_ge(s_sm, 16)
            pool.wait_ge(mx.s_mm[MT - 1], STEPS_MIX)
            pool.dma_start(ln_g, ln[:, 0]).then_inc(s_ln, 16)
            pool.dma_start(ln_b, ln[:, 1]).then_inc(s_ln, 16)
            pool.wait_ge(mx.s_wlo, GROUPS * WP + KT)
            pool.memset(zero, 0.0).then_inc(s_z, 1)
            pool.wait_ge(s_z, 1)
            pool.dma_start(x1_scr[ROWS:ROWS + P, :], zero).then_inc(s_zo, 16)
            pool.dma_start(acc_scr[ROWS:ROWS + P, :], zero).then_inc(s_zo, 16)

            pool.wait_ge(s_ln, 32)

            def tile(t, par, h):
                if isinstance(t, int) and t == NT - 1:
                    return
                pool.wait_ge(s_xg, t + 1)
                if not (isinstance(t, int) and t < 2):
                    pool.wait_ge(s_x1o[par], h * 16)
                    pool.wait_ge(s_tr, t - 1)
                    pool.wait_ge(s_ax, t - 1)
                pool.tensor_tensor(x1[par], s_sb[par], ln_b, ALU.add).then_inc(s_x1, 1)
            tiles(pool, tile)
            pool.wait_ge(s_zo, 32)

        @block.sync
        def _(sp):
            mix_sync(sp)

            def load(t, par, h, tail=False):
                n = TAIL if tail else P
                sp.wait_ge(s_ylo, t - 1)
                if tail:
                    sp.wait_ge(s_pad, 1)
                sp.dma_start(y_raw[par][:, :, 0:n],
                             y_scr[:, :, bass.ds(t * P, n)].rearrange("k p t -> p k t")).then_inc(s_yraw[par], 16)
                sp.wait_ge(s_s, t - 1)
                sp.dma_start(x_in[par], x_rows[bass.ds(t * P, P), :]).then_inc(s_x[par], 16)

            with sp.Fori(0, NT // 2 - 1) as h:
                for par in range(2):
                    load(h * 2 + (par + 2), par, h + 1)
            load(NT - 1, 0, NT // 2, tail=True)
            sp.wait_ge(mx.s_st_out, 16)
            for par in range(2):
                sp.wait_ge(s_x1o[par], 16 * (NT // 2 + 1 - par))
                sp.wait_ge(s_axo[par], 16 * (NT // 2 + 1 - par))

        @block.tensor
        def _(pe):
            def project(t, par, h):
                pe.wait_ge(s_ylo, t + 1)
                if not (isinstance(t, int) and t < 2):
                    pe.wait_ge(s_s, t - 1)
                else:
                    for read in ((mx.s_vb, mx.s_c), (mx.s_u, mx.s_ya))[par]:
                        pe.wait_ge(read, STEPS_MIX)
                for k in range(KT):
                    if isinstance(t, int) and t == 0:
                        pe.wait_ge(mx.s_wlo, GROUPS * WP + k + 1)
                    for n, (y, w) in enumerate(((y_hi, wo_hi), (y_hi, wo_lo), (y_lo, wo_hi))):
                        for f in range(2):
                            mm = pe.matmul(ps_m[par][:, f * 512:f * 512 + 512], y[par][:, k], w[:, k, f * 512:f * 512 + 512],
                                           start=(k == 0 and n == 0), stop=(k == KT - 1 and n == 2))
                mm.then_inc(s_m, 1)

            def turn(t, par):
                pe.wait_ge(s_x1, t + 1)
                if isinstance(t, int) and t == 0:
                    pe.wait_ge(mx.s_thi, STEPS_MIX)
                else:
                    pe.wait_ge(s_x1t, t)
                for k in range(KT):
                    mm = pe.transpose(ps_t[:, k], x1[par][:, k * P:(k + 1) * P], ident)
                mm.then_inc(s_tr, 1)

            def route(t, par):
                pe.wait_ge(s_x1t, t + 1)
                pe.wait_ge(s_lo, t + 1)
                for k in range(KT):
                    mm = pe.matmul(ps_l[:, 0:NR], x1_t[par][:, k], wr[:, k], start=(k == 0), stop=(k == KT - 1))
                mm.then_inc(s_l, 1)

            mix_tensor(pe)
            pe.wait_ge(s_c, 32)

            def tile(t, par, h):
                project(t, par, h)
                if not (isinstance(t, int) and t < 2):
                    route(t - 2, par)
                if not (isinstance(t, int) and t < 1):
                    turn(t - 1, 1 - par)
            tiles(pe, tile)
            route(NT - 2, (NT - 2) % 2)
            turn(NT - 1, (NT - 1) % 2)
            route(NT - 1, (NT - 1) % 2)

        @block.scalar
        def _(act):
            def split_y(t, par, h):
                act.wait_ge(s_yraw[par], h * 16 + 16)
                act.wait_ge(s_m, t - 1)
                act.activation(y_hi[par], y_raw[par], ACT.Copy).then_inc(s_yhi, 1)

            def turned(t, par):
                act.wait_ge(s_tr, t + 1)
                if not (isinstance(t, int) and t < 2):
                    act.wait_ge(s_lo, t)
                act.activation(x1_t[par], ps_t, ACT.Copy).then_inc(s_x1t, 1)

            def store_ax(t, par):
                act.wait_ge(s_ax, t + 1)
                act.dma_start(acc_scr[bass.ds(t * P, P), :], ax1[par]).then_inc(s_axo[par], 16)

            def tile(t, par, h, more=True):
                if more:
                    split_y(t + 2, par, h + 1)
                if not (isinstance(t, int) and t < 1):
                    store_ax(t - 1, 1 - par)
                    turned(t - 1, 1 - par)
                act.wait_ge(s_mv, t + 1)
                act.activation(std[:, par:par + 1], mv[:, par, 1:2], ACT.Sqrt, bias=eps[:]).then_inc(s_std, 1)
                act.wait_ge(s_nmr, t + 1)
                act.activation(s_sb[par], s_sb[par], ACT.Identity, scale=rstd[:, par:par + 1],
                               bias=nmr[:, par:par + 1]).then_inc(s_xn, 1)
                act.wait_ge(s_x1, t + 1)
                act.dma_start(x1_scr[bass.ds(t * P, P), :], x1[par]).then_inc(s_x1o[par], 16)
                if not (isinstance(t, int) and t < 2):
                    act.wait_ge(s_axo[par], h * 16)
                act.activation(ax1[par], x1[par], ACT.Copy, scale=ALPHA).then_inc(s_ax, 1)

            mix_scalar(act)
            tile(0, 0, 0)
            tile(1, 1, 0)
            with act.Fori(1, NT // 2 - 1) as h:
                tile(h * 2, 0, h)
                tile(h * 2 + 1, 1, h)
            tile(NT - 3, 0, NT // 2 - 1)
            tile(NT - 2, 1, NT // 2 - 1, more=False)
            tile(NT - 1, 0, NT // 2, more=False)
            store_ax(NT - 1, 0)
            turned(NT - 1, 0)

        @block.vector
        def _(dve):
            def split_y(t, par):
                dve.wait_ge(s_yhi, t + 1)
                dve.tensor_tensor(y_lo[par], y_raw[par], y_hi[par].bitcast(F32), ALU.subtract).then_inc(s_ylo, 1)

            def logits_out(t):
                dve.wait_ge(s_l, t + 1)
                dve.tensor_copy(logits[:, bass.ds(t, 1)].rearrange("p o n -> p (o n)"), ps_l[:, 0:NR]).then_inc(s_lo, 1)

            def tile(t, par, h, more=True, pad=False):
                dve.wait_ge(s_m, t + 1)
                dve.wait_ge(s_x[par], h * 16 + 16)
                if not (isinstance(t, int) and t < 2):
                    dve.wait_ge(s_x1, t - 1)
                for f in range(2):
                    c = slice(f * 512, f * 512 + 512)
                    ins = dve.scalar_tensor_tensor(out=s_sb[par][:, c], in0=x_in[par][:, c], scalar=ALPHA,
                                                   in1=ps_m[par][:, c], op0=ALU.mult, op1=ALU.add)
                ins.then_inc(s_s, 1)
                dve.wait_ge(s_s, t + 1)
                for f in range(2):
                    ins = dve.bn_stats(stats[:, par, f], s_sb[par][:, f * 512:f * 512 + 512])
                ins.then_inc(s_bn, 1)
                dve.wait_ge(s_bn, 1)
                dve.wait_ge(s_bn, t + 1)
                dve.bn_aggr(mv[:, par], stats[:, par]).then_inc(s_mv, 1)
                if pad:
                    dve.wait_ge(s_ylo, NT - 2)
                    dve.memset(y_raw[0], 0.0).then_inc(s_pad, 1)
                if more:
                    split_y(t + 2, par)
                dve.wait_ge(s_std, t + 1)
                dve.reciprocal(rstd[:, par:par + 1], std[:, par:par + 1]).then_inc(s_rstd, 1)
                dve.wait_ge(s_rstd, t + 1)
                dve.scalar_tensor_tensor(out=nmr[:, par:par + 1], in0=mv[:, par, 0:1], scalar=-1.0,
                                         in1=rstd[:, par:par + 1], op0=ALU.mult, op1=ALU.mult).then_inc(s_nmr, 1)
                if not (isinstance(t, int) and t < 2):
                    logits_out(t - 2)
                dve.wait_ge(s_xn, t + 1)
                dve.tensor_tensor(s_sb[par], s_sb[par], ln_g, ALU.mult).then_inc(s_xg, 1)
                if isinstance(t, int) and t == NT - 1:
                    dve.wait_ge(s_xg, NT)
                    dve.wait_ge(s_x1o[par], h * 16)
                    dve.wait_ge(s_tr, t - 1)
                    dve.wait_ge(s_ax, t - 1)
                    dve.tensor_tensor(x1[par], s_sb[par], ln_b, ALU.add).then_inc(s_x1, 1)
            dve.memset(eps[:], LN_EPS).then_inc(s_lo, 1)
            mix_vector(dve)
            dve.wait_ge(s_ln, 32)
            tile(0, 0, 0)
            tile(1, 1, 0)
            with dve.Fori(1, NT // 2 - 1) as h:
                tile(h * 2, 0, h)
                tile(h * 2 + 1, 1, h)
            tile(NT - 3, 0, NT // 2 - 1, pad=True)
            tile(NT - 2, 1, NT // 2 - 1, more=False)
            tile(NT - 1, 0, NT // 2, more=False)
            logits_out(NT - 2)
            logits_out(NT - 1)


class ExpertWeights:

    def __init__(self, nc, ctx):
        def sb(name, shape, dt=F32):
            return ctx.enter_context(nc.sbuf_tensor(name, shape, dt))

        def sem(name):
            return ctx.enter_context(nc.semaphore(name))

        self.w13_raw = sb("w13_raw", [P, KT, 2 * FE])
        self.w2_raw = sb("w2_raw", [P, FT, D])
        self.w13_hi = sb("w13_hi", [P, 2, KT, 2 * FE], F32R)
        self.w13_lo = sb("w13_lo", [P, 2, KT, 2 * FE], F32R)
        self.w2_hi = sb("w2_hi", [P, 2, FT, D], F32R)
        self.w2_lo = sb("w2_lo", [P, 2, FT, D], F32R)
        self.s_r13, self.s_r2 = sem("s_r13"), sem("s_r2")
        self.s_13hi, self.s_13lo = sem("s_13hi"), sem("s_13lo")
        self.s_2hi, self.s_2lo = sem("s_2hi"), sem("s_2lo")

    def half(self, tensor, at, i):
        return tensor[:, at, i * (KT // 2):(i + 1) * (KT // 2)].rearrange("p o k n -> p (o k) n")

    def raw_half(self, i):
        return self.w13_raw[:, i * (KT // 2):(i + 1) * (KT // 2)]

    def hi13(self, act, n, at):
        act.wait_ge(self.s_r13, n * 16 + 16)
        for i in range(2):
            act.activation(self.half(self.w13_hi, at, i), self.raw_half(i), ACT.Copy).then_inc(self.s_13hi, 1)

    def lo13(self, eng, n, at, halves=(0, 1)):
        for i in halves:
            eng.wait_ge(self.s_13hi, n * 2 + (i + 1))
            eng.tensor_tensor(self.half(self.w13_lo, at, i), self.raw_half(i),
                              self.half(self.w13_hi, at, i).bitcast(F32), ALU.subtract).then_inc(self.s_13lo, 1)

    def hi2(self, act, n, at):
        act.wait_ge(self.s_r2, n * 16 + 16)
        act.activation(self.w2_hi[:, at].rearrange("p o k n -> p (o k) n"), self.w2_raw[:], ACT.Copy).then_inc(self.s_2hi, 1)

    def lo2(self, eng, n, at):
        eng.wait_ge(self.s_2hi, n + 1)
        eng.tensor_tensor(self.w2_lo[:, at].rearrange("p o k n -> p (o k) n"), self.w2_raw[:],
                          self.w2_hi[:, at].rearrange("p o k n -> p (o k) n").bitcast(F32),
                          ALU.subtract).then_inc(self.s_2lo, 1)


def route_phase(nc, consts, logits, ids, gates, plan, ew, w13, w2, ln, ln2, consts_in, small):
    with ExitStack() as ctx:
        def sb(name, shape, dt=F32):
            return ctx.enter_context(nc.sbuf_tensor(name, shape, dt))

        def sem(name):
            return ctx.enter_context(nc.semaphore(name))

        t3 = [sb(f"t3_{i}", [P, NT, NG]) for i in range(4)]
        lg, q4, goh, e4 = t3
        gexp = sb("gexp", [P, NT, NG])
        e4b = sb("e4b", [P, NT, NE_G])
        oh = [sb(f"oh{i}", [P, NT, NE_G]) for i in range(2)]
        col = sb("col", [P, 10, NT])
        gmax, gsum, ggate, mx, m1, m2, ex, rec = (col[:, i] for i in range(8))
        wts = sb("wts", [P, TOPK, NT])
        a16 = [sb(f"a16_{i}", [P, NT, NG, NE_G]) for i in range(3)]
        big = sb("big", [P, NT, NG, NE_G])
        tot = sb("tot", [P, NE, NT])
        inc = sb("inc", [P, NE, NT])
        slot = sb("slot", [P, NT, NE])
        cmpc = sb("cmpc", [P, NE, NT])
        ecol = sb("ecol", [P, 4, NE])
        ntile, ecum, base = (ecol[:, i] for i in range(3))
        sl = sb("sl", [P, TOPK, NT])
        sli = sb("sli", [P, TOPK, NT], I32)
        shi_i = sb("shi_i", [P, TOPK, NT], I32)
        slo_i = sb("slo_i", [P, TOPK, NT], I32)
        shi = sb("shi", [P, TOPK, NT])
        slo = sb("slo", [P, TOPK, NT])
        at_lo = sb("at_lo", [P, TOPK, NT, P])
        at_hi = sb("at_hi", [P, TOPK, NT, 2, STEPS])
        hit = sb("hit", [P, TOPK, NT, STEPS])
        tab = sb("tab", [P, STEPS])
        cmps = sb("cmps", [1, STEPS, NE - 1])
        est = sb("est", [1, STEPS + 1])
        new = sb("new", [1, STEPS])
        pairs = sb("pairs", [1, 1], I32)
        ps_pos = ctx.enter_context(nc.psum_tensor("ps_pos", [P, 512], F32))
        ps_tot = ctx.enter_context(nc.psum_tensor("ps_tot", [P, 512], F32))
        ps_tab = ctx.enter_context(nc.psum_tensor("ps_tab", [P, 512], F32))

        s_dve = sem("s_rdve")
        s_dif = sem("s_rdif")
        s_con = sem("s_con")
        s_ln2 = sem("s_ln2")
        s_exp = sem("s_rexp")
        s_m2 = sem("s_rm2")
        s_wts = sem("s_rwts")
        s_asg = sem("s_rasg")
        s_cnt = sem("s_rcnt")
        s_hot = sem("s_rhot")
        s_hit = sem("s_rhit")
        s_hot1 = sem("s_rhot1")
        s_put = sem("s_rput")
        block = ctx.enter_context(nc.Block())
        count = [0]

        first = bass.ds(0, 1)

        @block.sync
        def _(sp):
            sp.dma_start(consts[:], consts_in).then_inc(s_con, 16)
            sp.dma_start(ew.w2_raw[:], w2[0]).then_inc(ew.s_r2, 16)
            sp.dma_start(ew.w13_raw[:], w13[0]).then_inc(ew.s_r13, 16)
            sp.dma_start(ln2, ln[:, 2:4]).then_inc(s_ln2, 16)
            sp.wait_ge(ew.s_2lo, 1)
            sp.dma_start(ew.w2_raw[:], w2[1]).then_inc(ew.s_r2, 16)
            sp.wait_ge(ew.s_13lo, 2)
            sp.dma_start(ew.w13_raw[:], w13[1]).then_inc(ew.s_r13, 16)
            sp.wait_ge(s_ln2, 16)

        @block.scalar
        def _(act):
            act.wait_ge(s_dif, 1)
            act.activation(gexp[:], lg[:], ACT.Exp).then_inc(s_exp, 1)
            act.wait_ge(s_m2, 1)
            act.activation(ex, m2, ACT.Exp).then_inc(s_exp, 1)
            ew.hi2(act, 0, first)
            ew.hi13(act, 0, first)

        @block.tensor
        def _(pe):
            a = a16[2][:].rearrange("p t g e -> p (t g e)")
            pe.wait_ge(s_con, 16)
            pe.wait_ge(s_asg, 1)
            pe.matmul(ps_pos[:, 0:NT * NE], consts[:, C_TRI:C_TRI + P], a, start=True, stop=True)
            pe.matmul(ps_tot[:, 0:NT * NE], consts[:, C_ONE:C_ONE + P], a, start=True, stop=True).then_inc(s_cnt, 1)

            for n, (c, tiles_of) in enumerate(PARTS):
                pe.wait_ge(s_hot, n + 1)
                pe.wait_ge(s_hot1, n + 1)
                for t in range(NT)[tiles_of]:
                    mm = pe.matmul(ps_tab[:, 0:2 * STEPS], at_lo[:, c, t], at_hi[:, c, t].rearrange("p a s -> p (a s)"),
                                   start=(c == 0 and t == 0), stop=(c == 1 and t == NT - 1))
            mm.then_inc(s_put, 1)

        def over(ap, m, n):
            return ap.unsqueeze(2).broadcast_to((P, m, n))

        def ramp(m, n):
            return consts[:, C_IO:C_IO + n].unsqueeze(1).broadcast_to((P, m, n))

        @block.gpsimd
        def _(pool):
            ew.lo13(pool, 0, first, (0,))
            for n, (c, at) in enumerate(PARTS):
                m = len(range(NT)[at])
                pool.wait_ge(s_hit, n + 1)
                tok = small[:, C_TOK - C_DEC:C_TOK - C_DEC + NT]
                pool.tensor_tensor(at_hi[:, c, at, 0], hit[:, c, at], over(tok[:, at], m, STEPS), ALU.mult)
                pool.tensor_tensor(at_hi[:, c, at, 1], hit[:, c, at], over(wts[:, c, at], m, STEPS), ALU.mult).then_inc(s_hot1, 1)

        @block.vector
        def _(dve):
            def then(ins):
                count[0] += 1
                ins.then_inc(s_dve, 1)
                dve.wait_ge(s_dve, count[0])

            def bc(ap, n):
                return ap.unsqueeze(2).broadcast_to((P, NT, n))

            dec = small[:, 0:NG].unsqueeze(1).broadcast_to((P, NT, NG))

            def first_max(out, diff):
                then(dve.scalar_tensor_tensor(out=q4[:], in0=diff, scalar=0.0, in1=dec, op0=ALU.is_ge, op1=ALU.mult))
                then(dve.tensor_reduce(mx, q4[:], AX.X, ALU.max))
                then(dve.tensor_tensor(out, q4[:], bc(mx, NG), ALU.is_equal))

            then(dve.tensor_reduce(gmax, logits[:, :, 0:NG], AX.X, ALU.max))
            dve.tensor_tensor(lg[:], logits[:, :, 0:NG], bc(gmax, NG), ALU.subtract).then_inc(s_dif, 1)
            dve.wait_ge(s_dif, 1)
            first_max(goh[:], lg[:])
            le = logits[:, :, NG:NR].rearrange("p t (g e) -> p t g e", g=NG)
            goh_b = goh[:].unsqueeze(3).broadcast_to((P, NT, NG, NE_G))
            then(dve.tensor_tensor(big[:], le, goh_b, ALU.mult))
            then(dve.tensor_reduce(e4[:], big[:].rearrange("p t g e -> p t e g"), AX.X, ALU.add))
            then(dve.tensor_reduce(m1, e4[:], AX.X, ALU.max))
            then(dve.tensor_tensor(e4[:], e4[:], bc(m1, NE_G), ALU.subtract))
            first_max(oh[0][:], e4[:])
            then(dve.scalar_tensor_tensor(out=e4b[:], in0=oh[0][:], scalar=-1e30, in1=e4[:], op0=ALU.mult, op1=ALU.add))
            dve.tensor_reduce(m2, e4b[:], AX.X, ALU.max).then_inc(s_m2, 1)
            dve.wait_ge(s_m2, 1)
            then(dve.tensor_tensor(e4b[:], e4b[:], bc(m2, NE_G), ALU.subtract))
            first_max(oh[1][:], e4b[:])
            then(dve.tensor_tensor(goh[:], goh[:], bc(small[:, C_VAL - C_DEC:C_VAL - C_DEC + NT], NG), ALU.mult))
            for c in range(TOPK):
                then(dve.tensor_tensor(a16[c][:], goh_b, oh[c][:].unsqueeze(2).broadcast_to((P, NT, NG, NE_G)), ALU.mult))
            dve.tensor_tensor(a16[2][:], a16[0][:], a16[1][:], ALU.add).then_inc(s_asg, 1)
            dve.wait_ge(s_exp, 2)
            dve.tensor_scalar(rec, ex, 1.0, None, ALU.add)
            then(dve.tensor_reduce(gsum, gexp[:], AX.X, ALU.add))
            dve.reciprocal(ggate, gsum)
            then(dve.reciprocal(rec, rec))
            then(dve.tensor_tensor(wts[:, 0], rec, ggate, ALU.mult))
            dve.tensor_tensor(wts[:, 1], wts[:, 0], ex, ALU.mult).then_inc(s_wts, 1)
            ew.lo2(dve, 0, first)
            dve.wait_ge(s_con, 16)
            dve.wait_ge(s_cnt, 1)
            then(dve.tensor_copy(tot[:], ps_tot[:, 0:NT * NE].rearrange("p (t e) -> p e t", e=NE)))
            flat = lambda x: x[:].rearrange("p e t -> p (e t)")
            then(dve.tensor_tensor_scan(flat(inc), consts[:, C_SEG:C_SEG + NT * NE], flat(tot), 0.0, ALU.mult, ALU.add))
            then(dve.tensor_tensor(tot[:], inc[:], tot[:], ALU.subtract))
            then(dve.tensor_tensor(cmpc[:], inc[:, :, NT - 1].unsqueeze(2).broadcast_to((P, NE, NT)),
                                   small[:, C_THR - C_DEC:C_THR - C_DEC + NT].unsqueeze(1).broadcast_to((P, NE, NT)), ALU.is_gt))
            then(dve.tensor_reduce(ntile, cmpc[:], AX.X, ALU.add))
            then(dve.tensor_scalar(ntile, ntile, 1.0, None, ALU.max))
            then(dve.tensor_tensor_scan(ecum, consts[:, C_ONE:C_ONE + NE], ntile, 0.0, ALU.mult, ALU.add))
            then(dve.tensor_tensor(base, ecum, ntile, ALU.subtract))
            then(dve.tensor_scalar(base, base, float(P), None, ALU.mult))
            then(dve.tensor_tensor(slot[:], tot[:].rearrange("p e t -> p t e"),
                                   ps_pos[:, 0:NT * NE].rearrange("p (t e) -> p t e", e=NE), ALU.add))
            then(dve.tensor_tensor(slot[:], slot[:], base.unsqueeze(1).broadcast_to((P, NT, NE)), ALU.add))
            for c in range(TOPK):
                then(dve.tensor_tensor(big[:], a16[c][:], slot[:].rearrange("p t (g e) -> p t g e", g=NG), ALU.mult))
                then(dve.tensor_reduce(sl[:, c], big[:].rearrange("p t g e -> p t (g e)"), AX.X, ALU.add))
                then(dve.tensor_tensor(sl[:, c], sl[:, c], small[:, C_INV - C_DEC:C_INV - C_DEC + NT], ALU.add))
            then(dve.tensor_copy(sli[:], sl[:]))
            dve.tensor_scalar(shi_i[:], sli[:], 7, None, ALU.logical_shift_right)
            then(dve.tensor_scalar(slo_i[:], sli[:], P - 1, None, ALU.bitwise_and))
            dve.tensor_copy(shi[:], shi_i[:])
            then(dve.tensor_copy(slo[:], slo_i[:]))
            dve.wait_ge(s_wts, 1)
            for n, (c, at) in enumerate(PARTS):
                m = len(range(NT)[at])
                dve.tensor_tensor(hit[:, c, at], ramp(m, STEPS), over(shi[:, c, at], m, STEPS), ALU.is_equal).then_inc(s_hit, 1)
                dve.tensor_tensor(at_lo[:, c, at], ramp(m, P), over(slo[:, c, at], m, P), ALU.is_equal).then_inc(s_hot, 1)
            dve.wait_ge(ew.s_13lo, 1)
            ew.lo13(dve, 0, first, (1,))
            then(dve.tensor_tensor(cmps[:], consts[0:1, C_IO:C_IO + STEPS].unsqueeze(2).broadcast_to((1, STEPS, NE - 1)),
                                   ecum[0:1, 0:NE - 1].unsqueeze(1).broadcast_to((1, STEPS, NE - 1)), ALU.is_ge))
            dve.memset(est[:, 0:1], -1.0)
            then(dve.tensor_reduce(est[:, 1:], cmps[:], AX.X, ALU.add))
            dve.tensor_copy(plan[:, 0], est[:, 1:])
            then(dve.tensor_scalar(pairs[:], ecum[0:1, NE - 1:NE], float(1 - NE), None, ALU.add))
            dve.tensor_scalar(plan[:, 2, 0:1], pairs[:], 1, None, ALU.logical_shift_right)
            then(dve.tensor_tensor(new[:], est[:, 1:], est[:, 0:STEPS], ALU.not_equal))
            dve.scalar_tensor_tensor(out=plan[:, 1], in0=est[:, 1:], scalar=float(NE - 1), in1=new[:],
                                     op0=ALU.is_lt, op1=ALU.mult)
            dve.wait_ge(s_put, 1)
            then(dve.tensor_scalar(tab[:], ps_tab[:, 0:STEPS], 0.0, consts[:, C_PAD:C_PAD + 1], ALU.is_equal, ALU.mult))
            dve.tensor_scalar(ids[:, STEPS:], consts[:, C_PAD:C_PAD + 1], -1.0, None, ALU.add)
            dve.scalar_tensor_tensor(out=ids[:, 0:STEPS], in0=ps_tab[:, 0:STEPS], scalar=-1.0, in1=tab[:], op0=ALU.add, op1=ALU.add)
            then(dve.tensor_copy(gates[:], ps_tab[:, STEPS:2 * STEPS]))


def experts_phase(nc, x1_scr, acc_scr, w13, w2, consts, ids, gates, plan, ew):
    with ExitStack() as ctx:
        def sb(name, shape, dt=F32):
            return ctx.enter_context(nc.sbuf_tensor(name, shape, dt))

        def sem(name):
            return ctx.enter_context(nc.semaphore(name))

        w13_hi, w13_lo, w2_hi, w2_lo = ew.w13_hi, ew.w13_lo, ew.w2_hi, ew.w2_lo
        s_13lo, s_2lo = ew.s_13lo, ew.s_2lo
        xg = sb("xg", [P, 2, D])
        xt_hi = sb("xt_hi", [P, 2, KT, P], F32R)
        xt_lo = sb("xt_lo", [P, 2, KT, P], F32R)
        sil = sb("sil", [P, FE])
        hid = sb("hid", [P, FE])
        ht_hi = sb("ht_hi", [P, FT, P], F32R)
        ht_lo = sb("ht_lo", [P, FT, P], F32R)
        out = sb("out_sb", [P, 2, D])
        id_g = sb("id_g", [P, 2], I32)
        id_s = sb("id_s", [P, 2], I32)
        ps_x = ctx.enter_context(nc.psum_tensor("ps_x", [P, KT, P], F32))
        ps_h = [ctx.enter_context(nc.psum_tensor(f"ps_h{i}", [P, 2 * FE], F32)) for i in range(2)]
        ps_ht = ctx.enter_context(nc.psum_tensor("ps_ht", [P, 4, P], F32))
        ps_o = [ctx.enter_context(nc.psum_tensor(f"ps_o{i}", [P, 512], F32)) for i in range(2)]

        s_id0, s_idg = sem("s_id0"), sem("s_idg")
        s_ids = sem("s_ids")
        s_xg = [sem(f"s_xg{i}") for i in range(2)]
        s_tx, s_xhi, s_xlo = sem("s_tx"), sem("s_xthi"), sem("s_xtlo")
        s_h, s_sil, s_hid = sem("s_hm"), sem("s_sil"), sem("s_hid")
        s_th, s_hhi, s_hlo = sem("s_th"), sem("s_hthi"), sem("s_htlo")
        s_o, s_oa, s_ov = sem("s_o"), sem("s_oa"), sem("s_ov")
        s_add = sem("s_add")
        block = ctx.enter_context(nc.Block())

        def steps(eng, emit):
            pairs = eng.value_load(plan[0:1, 2, 0:1], min_val=0, max_val=(STEPS - NE) // 2) + NE // 2
            emit(0, 0, 0, 2)
            emit(1, 1, 0, 2)
            with eng.Fori(1, STEPS // 2 - 1) as h:
                with eng.If(h < pairs - 1):
                    emit(h * 2, 0, h, 2)
                    emit(h * 2 + 1, 1, h, 2)
            emit(pairs * 2 - 2, 0, pairs - 1, 1)
            emit(pairs * 2 - 1, 1, pairs - 1, 0)
            return pairs * 2 - 1

        def early(s, n):
            return isinstance(s, int) and s < n

        @block.sync
        def _(sp):
            with sp.Fori(2, NE) as e:
                sp.wait_ge(s_13lo, e * 2)
                sp.dma_start(ew.w13_raw[:], w13[bass.ds(e, 1)].rearrange("o p k n -> p (o k) n")).then_inc(ew.s_r13, 16)
                sp.wait_ge(s_2lo, e)
                sp.dma_start(ew.w2_raw[:], w2[bass.ds(e, 1)].rearrange("o p k n -> p (o k) n")).then_inc(ew.s_r2, 16)

        @block.gpsimd
        def _(pool):
            def gather(s, par):
                if not early(s, 2):
                    pool.wait_ge(s_tx, s - 1)
                if early(s, 2):
                    pool.tensor_copy(id_g[:, par:par + 1], ids[:, s:s + 1]).then_inc(s_id0, 1)
                    pool.wait_ge(s_id0, s + 1)
                else:
                    pool.tensor_copy(id_g[:, par:par + 1], ids[:, bass.ds(s, 1)]).then_inc(s_idg, 1)
                    pool.wait_ge(s_idg, 1)
                    pool.wait_ge(s_idg, s - 1)
                pool.indirect_dma_start(xg[:, par], None, x1_scr,
                                        bass.IndirectOffsetOnAxis(id_g[:, par:par + 1], 0)).then_inc(s_xg[par], 16)

            def add(s, par):
                pool.wait_ge(s_add, s * 16)
                done = s + 1
                pool.wait_ge(s_oa, done)
                pool.tensor_copy(id_s[:, par:par + 1], ids[:, bass.ds(s, 1)]).then_inc(s_ids, 1)
                pool.wait_ge(s_ids, 1)
                pool.wait_ge(s_ids, done)
                pool.wait_ge(s_ov, done)
                pool.indirect_dma_start(acc_scr, bass.IndirectOffsetOnAxis(id_s[:, par:par + 1], 0),
                                        out[:, par], None, compute_op=ALU.add).then_inc(s_add, 16)

            def step(s, par, h, left):
                if left == 2:
                    gather(s + 3, 1 - par)
                if not early(s, 1):
                    add(s - 1, 1 - par)

            for s in range(3):
                gather(s, s % 2)
            last = steps(pool, step)
            add(last, 1)
            pool.wait_ge(s_xg[0], last * 8 + 24)
            pool.wait_ge(s_add, last * 16 + 16)

        @block.tensor
        def _(pe):
            def turn(s, par, h):
                pe.wait_ge(s_xg[par], h * 16 + 16)
                pe.wait_ge(s_xlo, s)
                for k in range(KT):
                    mm = pe.transpose(ps_x[:, k], xg[:, par, k * P:(k + 1) * P], consts[:, C_ID:C_ID + P])
                mm.then_inc(s_tx, 1)

            def output(s, expert):
                at = expert % 2
                pe.wait_ge(s_hlo, s + 1)
                pe.wait_ge(s_2lo, expert + 1)
                pe.wait_ge(s_oa, s)
                pe.wait_ge(s_ov, s)
                for k in range(FT):
                    for n, (x, w) in enumerate(((ht_hi, w2_hi), (ht_hi, w2_lo), (ht_lo, w2_hi))):
                        for f in range(2):
                            mm = pe.matmul(ps_o[f][:], x[:, k],
                                           w[:, bass.ds(at, 1), k, f * 512:f * 512 + 512].rearrange("p o n -> p (o n)"),
                                           start=(k == 0 and n == 0), stop=(k == FT - 1 and n == 2))
                mm.then_inc(s_o, 1)

            def step(s, par, h, left):
                expert = pe.value_load(plan[0:1, 0, bass.ds(s, 1)], min_val=0, max_val=NE - 1)
                at = expert % 2
                if left:
                    turn(s + 1, 1 - par, h if par == 0 else h + 1)
                pe.wait_ge(s_xlo, s + 1)
                pe.wait_ge(s_13lo, expert * 2 + 2)
                if not early(s, 2):
                    pe.wait_ge(s_hid, s - 1)
                for k in range(KT):
                    for n, (x, w) in enumerate(((xt_hi, w13_hi), (xt_hi, w13_lo), (xt_lo, w13_hi))):
                        mm = pe.matmul(ps_h[par][:], x[:, par, k], w[:, bass.ds(at, 1), k].rearrange("p o n -> p (o n)"),
                                       start=(k == 0 and n == 0), stop=(k == KT - 1 and n == 2))
                mm.then_inc(s_h, 1)
                if not early(s, 1):
                    output(s - 1, pe.value_load(plan[0:1, 0, bass.ds(s - 1, 1)], min_val=0, max_val=NE - 1))
                pe.wait_ge(s_hid, s + 1)
                for k in range(FT):
                    mm = pe.transpose(ps_ht[:, k], hid[:, k * P:(k + 1) * P], consts[:, C_ID:C_ID + P])
                mm.then_inc(s_th, 1)

            turn(0, 0, 0)
            last = steps(pe, step)
            output(last, pe.value_load(plan[0:1, 0, bass.ds(last, 1)], min_val=0, max_val=NE - 1))

        @block.scalar
        def _(act):
            def h_hi(s):
                act.wait_ge(s_th, s + 1)
                act.activation(ht_hi[:], ps_ht[:, 0:FT], ACT.Copy).then_inc(s_hhi, 1)

            def x_hi(s, par):
                act.wait_ge(s_tx, s + 1)
                if not early(s, 2):
                    act.wait_ge(s_h, s - 1)
                act.activation(xt_hi[:, par], ps_x[:], ACT.Copy).then_inc(s_xhi, 1)

            def out_half(s, par):
                act.wait_ge(s_o, s + 1)
                if not early(s, 1):
                    act.wait_ge(s_ids, s)
                act.activation(out[:, par, 0:512], ps_o[0][:], ACT.Copy).then_inc(s_oa, 1)

            def step(s, par, h, left):
                expert = act.value_load(plan[0:1, 0, bass.ds(s, 1)], min_val=0, max_val=NE - 1)
                split = act.value_load(plan[0:1, 1, bass.ds(s, 1)], min_val=0, max_val=1)
                at = bass.ds((expert + 1) % 2, 1)
                if not early(s, 1):
                    h_hi(s - 1)
                if left:
                    x_hi(s + 1, 1 - par)
                with act.If(split):
                    ew.hi13(act, expert + 1, at)
                act.wait_ge(s_h, s + 1)
                act.wait_ge(s_hid, s)
                act.activation(sil[:], ps_h[par][:, 0:FE], ACT.Silu).then_inc(s_sil, 1)
                if not early(s, 1):
                    out_half(s - 1, 1 - par)
                with act.If(split):
                    ew.hi2(act, expert + 1, at)
                act.wait_ge(s_sil, 1)
                act.wait_ge(s_sil, s + 1)

            x_hi(0, 0)
            last = steps(act, step)
            h_hi(last)
            out_half(last, 1)

        @block.vector
        def _(dve):
            def h_lo(s):
                dve.wait_ge(s_hhi, s + 1)
                dve.tensor_tensor(ht_lo[:], ps_ht[:, 0:FT], ht_hi[:].bitcast(F32), ALU.subtract).then_inc(s_hlo, 1)

            def x_lo(s, par):
                dve.wait_ge(s_xhi, s + 1)
                dve.tensor_tensor(xt_lo[:, par], ps_x[:], xt_hi[:, par].bitcast(F32), ALU.subtract).then_inc(s_xlo, 1)

            def out_half(s, par):
                dve.wait_ge(s_o, s + 1)
                if not early(s, 1):
                    dve.wait_ge(s_ids, s)
                dve.tensor_copy(out[:, par, 512:D], ps_o[1][:]).then_inc(s_ov, 1)

            def step(s, par, h, left):
                expert = dve.value_load(plan[0:1, 0, bass.ds(s, 1)], min_val=0, max_val=NE - 1)
                split = dve.value_load(plan[0:1, 1, bass.ds(s, 1)], min_val=0, max_val=1)
                at = bass.ds((expert + 1) % 2, 1)
                if not early(s, 1):
                    h_lo(s - 1)
                if left:
                    x_lo(s + 1, 1 - par)
                with dve.If(split):
                    ew.lo13(dve, expert + 1, at, (0,))
                dve.wait_ge(s_sil, s + 1)
                dve.wait_ge(s_th, s)
                dve.scalar_tensor_tensor(out=hid[:], in0=sil[:], scalar=gates[:, bass.ds(s, 1)],
                                         in1=ps_h[par][:, FE:2 * FE], op0=ALU.mult, op1=ALU.mult).then_inc(s_hid, 1)
                with dve.If(split):
                    ew.lo13(dve, expert + 1, at, (1,))
                if not early(s, 1):
                    out_half(s - 1, 1 - par)
                with dve.If(split):
                    ew.lo2(dve, expert + 1, at)
                dve.wait_ge(s_hid, 1)
                dve.wait_ge(s_hid, s + 1)

            x_lo(0, 0)
            last = steps(dve, step)
            h_lo(last)
            out_half(last, 1)


def finish_phase(nc, acc_scr, y_out, ln2):
    with ExitStack() as ctx:
        def sb(name, shape, dt=F32):
            return ctx.enter_context(nc.sbuf_tensor(name, shape, dt))

        def sem(name):
            return ctx.enter_context(nc.semaphore(name))

        v = sb("v", [P, NT, D])
        stats = sb("stats2", [P, NT, 2, 6])
        mv = sb("mv2", [P, NT, 2])
        std = sb("std2", [P, NT])
        rstd = sb("rstd2", [P, NT])
        nmr = sb("nmr2", [P, NT])
        eps = sb("eps2", [P, 1])
        s_in = [sem(f"s_fin{i}") for i in range(NT)]
        s_bn, s_mv, s_std, s_rstd, s_nmr = (sem(n) for n in ("s_bn2", "s_mv2", "s_std2", "s_rstd2", "s_nmr2"))
        s_xn, s_xg, s_y = sem("s_xn2"), sem("s_xg2"), sem("s_y2")
        s_out = sem("s_out2")
        block = ctx.enter_context(nc.Block())

        @block.sync
        def _(sp):
            for t in range(NT):
                sp.dma_start(v[:, t], acc_scr[t * P:(t + 1) * P, :]).then_inc(s_in[t], 16)
            for t in range(NT):
                n = P if t < NT - 1 else TAIL
                sp.wait_ge(s_y, t + 1)
                sp.dma_start(y_out[t * P:t * P + n, :], v[0:n, t]).then_inc(s_out, 16)
            sp.wait_ge(s_out, 16 * NT)

        @block.gpsimd
        def _(pool):
            for t in range(NT):
                pool.wait_ge(s_xg, t + 1)
                pool.tensor_tensor(v[:, t], v[:, t], ln2[:, 1], ALU.add).then_inc(s_y, 1)

        @block.scalar
        def _(act):
            for t in range(NT):
                act.wait_ge(s_mv, t + 1)
                act.activation(std[:, t:t + 1], mv[:, t, 1:2], ACT.Sqrt, bias=eps[:]).then_inc(s_std, 1)
                act.wait_ge(s_nmr, t + 1)
                act.activation(v[:, t], v[:, t], ACT.Identity, scale=rstd[:, t:t + 1],
                               bias=nmr[:, t:t + 1]).then_inc(s_xn, 1)

        @block.vector
        def _(dve):
            dve.memset(eps[:], LN_EPS)
            for t in range(NT):
                dve.wait_ge(s_in[t], 16)
                for f in range(2):
                    ins = dve.bn_stats(stats[:, t, f], v[:, t, f * 512:f * 512 + 512])
                ins.then_inc(s_bn, 1)
                dve.wait_ge(s_bn, t + 1)
                dve.bn_aggr(mv[:, t], stats[:, t]).then_inc(s_mv, 1)
                if t:
                    dve.wait_ge(s_xn, t)
                    dve.tensor_tensor(v[:, t - 1], v[:, t - 1], ln2[:, 0], ALU.mult).then_inc(s_xg, 1)
                dve.wait_ge(s_std, t + 1)
                dve.reciprocal(rstd[:, t:t + 1], std[:, t:t + 1]).then_inc(s_rstd, 1)
                dve.wait_ge(s_rstd, t + 1)
                dve.scalar_tensor_tensor(out=nmr[:, t:t + 1], in0=mv[:, t, 0:1], scalar=-1.0,
                                         in1=rstd[:, t:t + 1], op0=ALU.mult, op1=ALU.mult).then_inc(s_nmr, 1)
            dve.wait_ge(s_xn, NT)
            dve.tensor_tensor(v[:, NT - 1], v[:, NT - 1], ln2[:, 0], ALU.mult).then_inc(s_xg, 1)


def program(nc, x_t, x_rows, w_in, w_lru, chan, w_out, w_router, ln, w13, w2, consts_in, y_out, states):
    y_scr = nc.dram_tensor("y_scr", (KT, P, ROWS), F32, kind="Internal").ap()
    x1_scr = nc.dram_tensor("x1_scr", (ROWS + P, D), F32, kind="Internal").ap()
    acc_scr = nc.dram_tensor("acc_scr", (ROWS + P, D), F32, kind="Internal").ap()
    with (nc.sbuf_tensor("logits", [P, NT, NR], F32) as logits, nc.sbuf_tensor("small", [P, NSMALL], F32) as small):
        mix_project_phase(nc, x_t, w_in, w_lru, chan, y_scr, states, x_rows, w_out, w_router, ln, consts_in,
                          x1_scr, acc_scr, logits, small)
        with (nc.sbuf_tensor("consts_sb", [P, NCONST], F32) as consts, nc.sbuf_tensor("ids", [P, STEPS + 1], I32) as ids, nc.sbuf_tensor("gates", [P, STEPS], F32) as gates,
              nc.sbuf_tensor("plan", [1, 3, STEPS], I32) as plan, nc.sbuf_tensor("ln2_sb", [P, 2, D], F32) as ln2):
            with ExitStack() as ctx:
                ew = ExpertWeights(nc, ctx)
                route_phase(nc, consts, logits, ids, gates, plan, ew, w13, w2, ln, ln2[:], consts_in, small)
                experts_phase(nc, x1_scr, acc_scr, w13, w2, consts, ids, gates, plan, ew)
            finish_phase(nc, acc_scr, y_out, ln2)


def lay_out(inputs):
    import numpy as np
    a = {k: np.asarray(v) for k, v in inputs.items()}
    x = np.zeros((ROWS, D), np.float32)
    x[:SEQ], x[SEQ:TOK] = a["x_prompt"][0], a["x_sample"][0]
    out = {"x_rows": x}
    out["x_t"] = x[:TOK].reshape(TOK, KT, P).transpose(2, 1, 0)
    w = a["w_in"][0].reshape(KT, P, 5, GROUPS, P)[:, :, [3, 1, 2, 0, 4]]
    out["w_in"] = w.transpose(3, 2, 1, 0, 4).reshape(GROUPS * MT, P, KT, P)
    lru = np.zeros((GROUPS, P, 2, P), np.float32)
    half = P // 2
    for g, name in enumerate(("lru_wa", "lru_wx")):
        for head in range(2 * GROUPS):
            s = half * (head % 2)
            lru[head // 2, s:s + half, g, s:s + half] = a[name][0, head]
    out["w_lru"] = lru
    cols = [*a["conv_a_w"][0], *a["conv_b_w"][0], a["conv_b_bias"][0], a["lru_ba"][0], a["lru_bx"][0],
            a["lru_lambda"][0], *a["state_conv_a"][0, 0], *a["state_conv_b"][0, 0], a["state_lru_h"][0, 0]]
    out["chan"] = np.stack(cols, -1).reshape(GROUPS, P, NCOL).transpose(1, 0, 2)
    out["w_out"] = a["w_out"][0].reshape(KT, P, D).transpose(1, 0, 2)
    wr = np.concatenate([a["w_router_group"][0], a["w_router_expert"][0]], -1)
    out["w_router"] = wr.reshape(KT, P, NR).transpose(1, 0, 2)
    out["ln"] = np.broadcast_to(np.stack([a[n][0] for n in ("ln1_g", "ln1_b", "ln2_g", "ln2_b")]), (P, 4, D))
    w13 = np.concatenate([a["moe_w1"][0], a["moe_w3"][0]], -1)
    out["w13"] = w13.reshape(NE, KT, P, 2 * FE).transpose(0, 2, 1, 3)
    out["w2"] = a["moe_w2"][0].reshape(NE, FT, P, D).transpose(0, 2, 1, 3)
    out["consts"] = constants(np)
    return out


def constants(np):
    c = np.zeros((P, NCONST), np.float32)
    p = np.arange(P)
    c[:, C_ID:C_ID + P] = np.eye(P)
    c[:, C_TRI:C_TRI + P] = p[:, None] < p[None]
    c[:, C_ONE:C_ONE + P] = 1
    c[:, C_IO:C_IO + P] = p
    c[:, C_DEC:C_DEC + NG] = NG - np.arange(NG)
    c[:, C_THR:C_THR + NT] = P * np.arange(NT)
    token = np.arange(NT) * P + p[:, None]
    c[:, C_TOK:C_TOK + NT] = token + 1
    c[:, C_VAL:C_VAL + NT] = token < TOK
    c[:, C_INV:C_INV + NT] = (token >= TOK) * 2.0 ** 17
    c[:, C_SEG:C_SEG + NT * NE] = np.arange(NT * NE) % NT != 0
    c[:, C_PAD] = ROWS + p + 1
    return c


def states_of(s):
    rows = s.transpose(2, 1, 0).reshape(NST, GROUPS * P)
    return [rows[SA_P:SA_P + 2].reshape(1, 1, 2, -1), rows[SB_P:SB_P + 3].reshape(1, 1, 3, -1), rows[SH_P].reshape(1, 1, -1),
            rows[SA_S:SA_S + 2].reshape(1, 1, 2, -1), rows[SB_S:SB_S + 3].reshape(1, 1, 3, -1), rows[SH_S].reshape(1, 1, -1)]


_INS = ("x_t", "x_rows", "w_in", "w_lru", "chan", "w_out", "w_router", "ln", "w13", "w2", "consts")
_OUTS = (("y_out", (TOK, D)), ("states", (P, GROUPS, NST)))


def kernel(**inputs):
    import numpy as np
    from concourse import bacc
    from concourse.bass_utils import run_bass_kernel_spmd

    laid = lay_out(inputs)
    nc = bacc.Bacc("TRN2", target_bir_lowering=False, num_devices=1)
    arrays = {f"in_{n}": np.ascontiguousarray(laid[n]) for n in _INS}
    args = [nc.dram_tensor(f"in_{n}", arrays[f"in_{n}"].shape, F32, kind="ExternalInput").ap() for n in _INS]
    args += [nc.dram_tensor(f"out_{n}", shape, F32, kind="ExternalOutput").ap() for n, shape in _OUTS]
    program(nc, *args)
    got = run_bass_kernel_spmd(nc, [arrays], core_ids=[0]).results[0]
    y = got["out_y_out"]
    return (y[:SEQ].reshape(1, SEQ, D), y[SEQ:].reshape(1, DEC, D), *states_of(got["out_states"]))
```
